# Optimizing a Trainium2 kernel written in Bass

```python
import math
import jax, jax.numpy as jnp
from jax import lax
import numpy as np

D_MODEL = 1024
BATCH = 1
SEQ = 512
DEPTH = 1
DEC_BATCH = 8
DEC_SEQ = 4
PAST_LEN = 4096
PAGE_SIZE = 128

N_HEADS_M = 4
HEAD_DIM_M = 256
D_MLSTM = N_HEADS_M * HEAD_DIM_M
MLSTM_CHUNK = 64
POOL_WINDOWS = (2, 4, 8, 16)
N_POOL_GROUPS = 4
POOL_GROUP_DIM = 128
D_POOL = N_POOL_GROUPS * POOL_GROUP_DIM
POOL_BUF = 15
N_EXPERTS = 16
N_EXPERT_GROUPS = 4
EXPERTS_PER_GROUP = N_EXPERTS // N_EXPERT_GROUPS
TOP_K = 2
D_EXPERT = 512
N_IN = 4 * D_MLSTM + 2 * N_HEADS_M + D_POOL + 2 * D_MODEL
ALPHA = (2 * DEPTH) ** 0.25
BETA = (8 * DEPTH) ** -0.25
LN_EPS = 1e-5

kernel_name = "xlstm_pool_moe_hybrid_step"

def _layer_norm(x, g, b):
    xf = x.astype(jnp.float32)
    mu = jnp.mean(xf, -1, keepdims=True)
    var = jnp.mean(jnp.square(xf - mu), -1, keepdims=True)
    y = (xf - mu) * lax.rsqrt(var + LN_EPS) * g.astype(jnp.float32) + b.astype(jnp.float32)
    return y.astype(x.dtype)

def _mlstm_chunk(carry, inp):
    c_prev, n_prev, m_prev = carry
    q, k, v, li, lf = inp
    L = q.shape[2]
    b = jnp.cumsum(lf, axis=-1)
    causal = jnp.tril(jnp.ones((L, L), dtype=bool))
    d = jnp.where(causal, b[..., :, None] - b[..., None, :] + li[..., None, :], -jnp.inf)
    inter = b + m_prev[..., None]
    m_t = jnp.maximum(inter, jnp.max(d, -1))
    s_inter = jnp.exp(inter - m_t)
    qk = jnp.einsum('bhtd,bhsd->bhts', q, k) * jnp.exp(d - m_t[..., None])
    num = s_inter[..., None] * jnp.einsum('bhtd,bhde->bhte', q, c_prev) + jnp.einsum('bhts,bhse->bhte', qk, v)
    den = s_inter * jnp.einsum('bhtd,bhd->bht', q, n_prev) + jnp.sum(qk, -1)
    h = num / jnp.maximum(jnp.abs(den), jnp.exp(-m_t))[..., None]
    b_last = b[..., -1]
    d_last = b_last[..., None] - b + li
    inter_last = b_last + m_prev
    m_new = jnp.maximum(inter_last, jnp.max(d_last, -1))
    w_last = jnp.exp(d_last - m_new[..., None])
    s_last = jnp.exp(inter_last - m_new)
    c_new = s_last[..., None, None] * c_prev + jnp.einsum('bhs,bhsd,bhse->bhde', w_last, k, v)
    n_new = s_last[..., None] * n_prev + jnp.einsum('bhs,bhsd->bhd', w_last, k)
    return (c_new, n_new, m_new), h

def _to_chunks(a, n_chunks, chunk):
    a = jnp.moveaxis(a, 2, 1)
    a = a.reshape(a.shape[:2] + (n_chunks, chunk) + a.shape[3:])
    return jnp.moveaxis(a, 2, 0)

def _mlstm(q, k, v, li, lf, c0, n0, m0):
    B, T, H, _ = q.shape
    chunk = math.gcd(T, MLSTM_CHUNK)
    nc = T // chunk
    xs = (_to_chunks(q, nc, chunk), _to_chunks(k, nc, chunk), _to_chunks(v, nc, chunk),
          _to_chunks(li, nc, chunk), _to_chunks(lf, nc, chunk))
    (c1, n1, m1), h = lax.scan(_mlstm_chunk, (c0, n0, m0), xs)
    h = jnp.moveaxis(h, 0, 2).reshape(B, H, T, HEAD_DIM_M)
    return jnp.swapaxes(h, 1, 2), c1, n1, m1

def _causal_pool(u, buf, start):
    B, T, _ = u.shape
    ext = jnp.concatenate([buf.astype(jnp.float32), u.astype(jnp.float32)], axis=1)
    csum = jnp.concatenate([jnp.zeros((B, 1, D_POOL), jnp.float32), jnp.cumsum(ext, axis=1)], axis=1)
    uf = ext[:, POOL_BUF:]
    pos = start + jnp.arange(T)
    off = POOL_BUF + 1
    groups = []
    for g, w in enumerate(POOL_WINDOWS):
        sl = slice(g * POOL_GROUP_DIM, (g + 1) * POOL_GROUP_DIM)
        wsum = csum[:, off:off + T, sl] - csum[:, off - w:off - w + T, sl]
        cnt = jnp.minimum(pos + 1, w).astype(jnp.float32)
        groups.append(wsum / cnt[None, :, None] - uf[..., sl])
    return jnp.concatenate(groups, axis=-1), ext[:, -POOL_BUF:]

def _moe(x, w_router, b_router, w_e_gate, w_e_up, w_e_down):
    B, T, D = x.shape
    xt = x.reshape(B * T, D)
    probs = jax.nn.softmax((xt @ w_router).astype(jnp.float32) + b_router.astype(jnp.float32), axis=-1)
    gscore = jnp.sum(lax.top_k(probs.reshape(-1, N_EXPERT_GROUPS, EXPERTS_PER_GROUP), TOP_K)[0], -1)
    gsel = jnp.argmax(gscore, axis=-1)
    in_group = (jnp.arange(N_EXPERTS) // EXPERTS_PER_GROUP)[None, :] == gsel[:, None]
    vals, idx = lax.top_k(jnp.where(in_group, probs, -1.0), TOP_K)
    wts = vals / jnp.sum(vals, -1, keepdims=True)
    gate = jnp.sum(jax.nn.one_hot(idx, N_EXPERTS, dtype=jnp.float32) * wts[..., None], axis=1)
    h = jax.nn.silu(jnp.einsum('nd,edf->nef', xt, w_e_gate)) * jnp.einsum('nd,edf->nef', xt, w_e_up)
    h = h * gate[..., None].astype(h.dtype)
    return jnp.einsum('nef,efd->nd', h, w_e_down).reshape(B, T, D)

def _layer(x, c0, n0, m0, buf, start, w_in, b_gate, hn_gain, w_pool, pool_scale, w_proj_a, w_proj_b,
           w_out, ln1_g, ln1_b, ln2_g, ln2_b, w_router, b_router, w_e_gate, w_e_up, w_e_down):
    B, T, _ = x.shape
    f32 = jnp.float32
    z = x @ w_in
    cuts = [D_MLSTM, 2 * D_MLSTM, 3 * D_MLSTM, 4 * D_MLSTM, 4 * D_MLSTM + N_HEADS_M,
            4 * D_MLSTM + 2 * N_HEADS_M, 4 * D_MLSTM + 2 * N_HEADS_M + D_POOL,
            4 * D_MLSTM + 2 * N_HEADS_M + D_POOL + D_MODEL]
    q, k, v, o, gi, gf, u, ga, gb = jnp.split(z, cuts, axis=-1)
    q = q.astype(f32).reshape(B, T, N_HEADS_M, HEAD_DIM_M)
    k = k.astype(f32).reshape(B, T, N_HEADS_M, HEAD_DIM_M) * HEAD_DIM_M ** -0.5
    v = v.astype(f32).reshape(B, T, N_HEADS_M, HEAD_DIM_M)
    li = gi.astype(f32) + b_gate[:N_HEADS_M].astype(f32)
    lf = jax.nn.log_sigmoid(gf.astype(f32) + b_gate[N_HEADS_M:].astype(f32))
    h, c1, n1, m1 = _mlstm(q, k, v, li, lf, c0.astype(f32), n0.astype(f32), m0.astype(f32))
    mu = jnp.mean(h, -1, keepdims=True)
    var = jnp.mean(jnp.square(h - mu), -1, keepdims=True)
    h = (h - mu) * lax.rsqrt(var + LN_EPS) * hn_gain.astype(f32)
    y_a = (jax.nn.sigmoid(o) * h.reshape(B, T, D_MLSTM).astype(x.dtype)) @ w_proj_a
    pooled, buf_new = _causal_pool(u, buf, start)
    pooled = jnp.einsum('btgc,gce->btge', pooled.reshape(B, T, N_POOL_GROUPS, POOL_GROUP_DIM).astype(x.dtype), w_pool)
    y_b = (pooled.reshape(B, T, D_POOL) * pool_scale) @ w_proj_b
    mix = jax.nn.sigmoid(ga) * y_a + jax.nn.sigmoid(gb) * y_b
    x = _layer_norm(ALPHA * x + mix @ w_out, ln1_g, ln1_b)
    x = _layer_norm(ALPHA * x + _moe(x, w_router, b_router, w_e_gate, w_e_up, w_e_down), ln2_g, ln2_b)
    return x, c1, n1, m1, buf_new

def _trunk(x, c_all, n_all, m_all, buf_all, start, w_in, b_gate, hn_gain, w_pool, pool_scale, w_proj_a,
           w_proj_b, w_out, ln1_g, ln1_b, ln2_g, ln2_b, w_router, b_router, w_e_gate, w_e_up, w_e_down):
    cs, ns, ms, bs = [], [], [], []
    for l in range(DEPTH):
        x, c1, n1, m1, b1 = _layer(x, c_all[l], n_all[l], m_all[l], buf_all[l], start, w_in[l], b_gate[l],
                                   hn_gain[l], w_pool[l], pool_scale[l], w_proj_a[l], w_proj_b[l], w_out[l],
                                   ln1_g[l], ln1_b[l], ln2_g[l], ln2_b[l], w_router, b_router,
                                   w_e_gate[l], w_e_up[l], w_e_down[l])
        cs.append(c1)
        ns.append(n1)
        ms.append(m1)
        bs.append(b1)
    return x, jnp.stack(cs), jnp.stack(ns), jnp.stack(ms), jnp.stack(bs)

def setup_inputs(seed: int = 0) -> dict:
    key = jax.random.key(seed)
    ks = jax.random.split(key, 24)
    nrm = jax.random.normal
    H, dh = N_HEADS_M, HEAD_DIM_M
    forget_bias = jnp.linspace(3.0, 6.0, H)[None, :] + 0.1 * nrm(ks[7], (DEPTH, H))
    input_bias = 0.1 * nrm(ks[8], (DEPTH, H))
    return {
        "x_prompt": nrm(ks[0], (BATCH, SEQ, D_MODEL), jnp.float32),
        "x_sample": nrm(ks[1], (DEC_BATCH, DEC_SEQ, D_MODEL), jnp.float32),
        "state_C": nrm(ks[2], (DEPTH, DEC_BATCH, H, dh, dh), jnp.float32) * dh ** -0.5,
        "state_n": 0.5 * nrm(ks[3], (DEPTH, DEC_BATCH, H, dh), jnp.float32),
        "state_m": 0.5 * nrm(ks[4], (DEPTH, DEC_BATCH, H), jnp.float32),
        "state_pool": nrm(ks[5], (DEPTH, DEC_BATCH, POOL_BUF, D_POOL), jnp.float32),
        "w_in": nrm(ks[6], (DEPTH, D_MODEL, N_IN), jnp.float32) * D_MODEL ** -0.5,
        "b_gate": jnp.concatenate([input_bias, forget_bias], axis=-1).astype(jnp.float32),
        "hn_gain": 1.0 + 0.02 * nrm(ks[9], (DEPTH, H, dh), jnp.float32),
        "w_pool": nrm(ks[10], (DEPTH, N_POOL_GROUPS, POOL_GROUP_DIM, POOL_GROUP_DIM), jnp.float32) * POOL_GROUP_DIM ** -0.5,
        "pool_scale": 1.0 + 0.1 * nrm(ks[11], (DEPTH, D_POOL), jnp.float32),
        "w_proj_a": nrm(ks[12], (DEPTH, D_MLSTM, D_MODEL), jnp.float32) * D_MLSTM ** -0.5,
        "w_proj_b": nrm(ks[13], (DEPTH, D_POOL, D_MODEL), jnp.float32) * D_POOL ** -0.5,
        "w_out": nrm(ks[14], (DEPTH, D_MODEL, D_MODEL), jnp.float32) * (BETA * D_MODEL ** -0.5),
        "ln1_g": 1.0 + 0.02 * nrm(ks[15], (DEPTH, D_MODEL), jnp.float32),
        "ln1_b": 0.02 * nrm(ks[16], (DEPTH, D_MODEL), jnp.float32),
        "ln2_g": 1.0 + 0.02 * nrm(ks[17], (DEPTH, D_MODEL), jnp.float32),
        "ln2_b": 0.02 * nrm(ks[18], (DEPTH, D_MODEL), jnp.float32),
        "w_router": nrm(ks[19], (D_MODEL, N_EXPERTS), jnp.float32) * D_MODEL ** -0.5,
        "b_router": 0.01 * nrm(ks[20], (N_EXPERTS,), jnp.float32),
        "w_e_gate": nrm(ks[21], (DEPTH, N_EXPERTS, D_MODEL, D_EXPERT), jnp.float32) * D_MODEL ** -0.5,
        "w_e_up": nrm(ks[22], (DEPTH, N_EXPERTS, D_MODEL, D_EXPERT), jnp.float32) * D_MODEL ** -0.5,
        "w_e_down": nrm(ks[23], (DEPTH, N_EXPERTS, D_EXPERT, D_MODEL), jnp.float32) * (BETA * D_EXPERT ** -0.5),
    }

def reference(x_prompt, x_sample, state_C, state_n, state_m, state_pool, w_in, b_gate, hn_gain, w_pool,
              pool_scale, w_proj_a, w_proj_b, w_out, ln1_g, ln1_b, ln2_g, ln2_b, w_router, b_router,
              w_e_gate, w_e_up, w_e_down):
    f32 = jnp.float32
    bp = x_prompt.shape[0]
    c0 = jnp.zeros((DEPTH, bp, N_HEADS_M, HEAD_DIM_M, HEAD_DIM_M), f32)
    n0 = jnp.zeros((DEPTH, bp, N_HEADS_M, HEAD_DIM_M), f32)
    m0 = jnp.zeros((DEPTH, bp, N_HEADS_M), f32)
    buf0 = jnp.zeros((DEPTH, bp, POOL_BUF, D_POOL), f32)
    y_prompt, c_p, n_p, m_p, pool_p = _trunk(
        x_prompt, c0, n0, m0, buf0, 0, w_in, b_gate, hn_gain, w_pool, pool_scale, w_proj_a, w_proj_b,
        w_out, ln1_g, ln1_b, ln2_g, ln2_b, w_router, b_router, w_e_gate, w_e_up, w_e_down)
    y_sample, c_s, n_s, m_s, pool_s = _trunk(
        x_sample, state_C, state_n, state_m, state_pool, PAST_LEN, w_in, b_gate, hn_gain, w_pool, pool_scale,
        w_proj_a, w_proj_b, w_out, ln1_g, ln1_b, ln2_g, ln2_b, w_router, b_router, w_e_gate, w_e_up, w_e_down)
    return (y_prompt, y_sample,
            c_p.astype(state_C.dtype), n_p.astype(state_n.dtype), m_p.astype(state_m.dtype), pool_p.astype(state_pool.dtype),
            c_s.astype(state_C.dtype), n_s.astype(state_n.dtype), m_s.astype(state_m.dtype), pool_s.astype(state_pool.dtype))


_drawn_inputs = setup_inputs


def setup_inputs(seed=0):
    import zlib

    import numpy as np

    out = dict(_drawn_inputs(seed))
    spreads = {}
    factors = {}
    for name, (base, spread) in spreads.items():
        noise = np.random.default_rng([zlib.crc32(name.encode()), seed]).standard_normal(out[name].shape)
        drawn = base * np.exp(spread * noise) if base else spread * noise
        out[name] = __import__('jax').numpy.asarray(drawn.astype(out[name].dtype))
    for name, factor in factors.items():
        out[name] = (out[name] * factor).astype(out[name].dtype)
    return out
```

```python
from contextlib import ExitStack

import concourse.bass as bass
from concourse import mybir

ALU = mybir.AluOpType
ACT = mybir.ActivationFunctionType
F32 = mybir.dt.float32
F32R = mybir.dt.float32r
BF16 = mybir.dt.bfloat16
I32 = mybir.dt.int32
U32 = mybir.dt.uint32
AX = mybir.AxisListType

P = 128
DM = 1024
SEQ, DB, DT = 512, 8, 4
NS = DB * DT
N = SEQ + NS
PT = SEQ // P
NT = PT + 1
HALF = N // 2
H, DH = 4, 256
NG, GD, BUF = 4, 128, 15
NE, EG, DE = 16, 4, 512
KT = DM // P
VW = DH + 2
ALPHA = 2.0 ** 0.25
EPS = 1e-5
FAR = -1e30
EXT = BUF + SEQ + DB * (BUF + DT)
XTRA = 8
ROWS = [P] * PT + [NS]

CONST = {}


def _const_columns():
    at = 0
    for name, width in (("ident", P), ("causal", P), ("causal_s", NS), ("seq_of", DB * NS), ("head_sel", H * P),
                        ("tok_seq", DB), ("first16", NG * 16), ("before", P), ("ones", P), ("slot", P),
                        ("tokid", NT * 2), ("expert", NE), ("valid", NT), ("block", XTRA), ("half", NT)):
        CONST[name] = (at, width)
        at += width
    return at


CW = _const_columns()

C_O, C_U, C_O2, C_PB, C_MIX, C_WO, C_MOE = 12, 14, 16, 18, 20, 32, 36
RAW_SLOTS, SPLIT_SLOTS, MOE_SLOTS = 3, 3, 6
CHUNK = 2048

J_X, J_LI, J_LF, J_BM, J_HEAD, J_O, J_U, J_O2, J_WP, J_PB, J_MIX, J_WO, J_XT = (
    0, 5, 6, 7, 11, 43, 47, 51, 55, 59, 67, 91, 99)
PER_HEAD, PER_MIX = 8, 6
T_COL, T_SIL, T_N, T_HEAD, T_POOL, T_PREV, T_POUT, T_NOUT, T_LOGIT, T_POS, T_CNT, T_IDX = (
    0, 1, 2, 3, 51, 52, 53, 54, 55, 56, 57, 58)
T_PER_HEAD = 12
H_PER_HEAD = 18
PER_DVE_HEAD = 22


class Steps:

    def __init__(self, sem):
        self.sem, self.base, self.count, self.per, self.turn = sem, 0, 0, 0, 0

    def value(self):
        return self.turn * self.per + (self.base + self.count) if self.per else self.base + self.count

    def mark(self, ins):
        ins.then_inc(self.sem, 1)
        self.count += 1
        return self.value()

    def loop(self, turn, per):
        self.base, self.count, self.per, self.turn = self.base + self.count, 0, per, turn

    def end(self, turns):
        assert self.count == self.per, (self.count, self.per)
        self.base, self.count, self.per, self.turn = self.base + self.per * turns, 0, 0, 0


def build(nc, consts, x_prompt, x_sample, state_C, state_n, state_m, state_pool, w_in, b_gate, hn_gain, w_pool,
          pool_scale, w_proj_a, w_proj_b, w_out, ln1_g, ln1_b, ln2_g, ln2_b, w_router, b_router, w_e_gate, w_e_up,
          w_e_down, y_prompt, y_sample, C_prompt, n_prompt, m_prompt, pool_prompt, C_sample, n_sample, m_sample,
          pool_sample):
    ctx = ExitStack()
    sems = {}

    def sem(name):
        sems[name] = ctx.enter_context(nc.semaphore(name))
        return sems[name]

    x1_rows = nc.dram_tensor("x1_rows", [N, DM], F32).ap()
    y_slots = nc.dram_tensor("y_slots", [(NE + XTRA) * P, DM], F32).ap()

    at0 = (nc.sbuf_base + 63) // 64 * 64
    limit = nc.sbuf_usable_end
    cursor = [at0]
    WIDTH = {F32: 4, F32R: 4, BF16: 2, I32: 4, U32: 4}

    def place(name, shape, dt, offset):
        return nc.alloc_sbuf_tensor_at(name, shape, dt, offset=offset)

    def size(shape, dt=F32):
        n = WIDTH[dt]
        for s in shape[1:]:
            n *= s
        return (n + 31) // 32 * 32

    def keep(name, shape, dt=F32):
        t = place(name, shape, dt, cursor[0])
        cursor[0] += size(shape, dt)
        return t

    def region(nbytes):
        start = cursor[0]
        cursor[0] += nbytes
        return start

    def lay(start, end, *items):
        out = []
        for name, shape, dt in items:
            out.append(place(name, shape, dt, start))
            start += size(shape, dt)
        assert start <= end, (items[-1][0], start - end)
        return out

    cst = keep("cst", [P, CW])

    def const(name, rows=P):
        a, w = CONST[name]
        return cst[0:rows, a:a + w]

    wg_raw = keep("wg_raw", [P, KT, 8])
    bias_g = keep("bias_g", [H, 2])
    m_prev = keep("m_prev", [H, DB])
    sil = keep("sil", [H, NS + DB])
    col = keep("col", [P, 3, NT, H])
    sb40 = keep("sb40", [P, H, NS + DB])
    wm = keep("wm", [NS, H, DB])
    gain = keep("gain", [P, KT])
    pscale = keep("pscale", [P, NG])
    nn = keep("nn", [NS, DH])
    ntr = keep("ntr", [P, 2, DB, H])
    ch = keep("ch", [P, 32])
    ncols = keep("ncols", [P, 72])
    nrows = keep("nrows", [72, P])
    held = keep("held", [1, 1])
    rsx = keep("rsx", [P, 1])
    den = keep("den", [P, 2, NT])
    hst = keep("hst", [P, NT, 6])
    hmv = keep("hmv", [P, NT, 2])
    hve = keep("hve", [P, NT])
    hrs = keep("hrs", [P, NT])
    hnm = keep("hnm", [P, NT])
    brt = keep("brt", [P, NE])
    wr = keep("wr", [P, KT, NE])
    mout = keep("mout", [H, DB + 1])
    lst = keep("lst", [P, NT, 2, 6])
    split_hi = keep("split_hi", [P, SPLIT_SLOTS, CHUNK], F32R)
    split_lo = keep("split_lo", [P, SPLIT_SLOTS, CHUNK], F32R)
    raw = keep("raw", [P, RAW_SLOTS, CHUNK])
    XW = KT * N + 96
    r_xt = region(2 * XW * 4)
    r_ht = region(KT * N * 4)
    r1 = region(73088)
    end = cursor[0]
    assert end <= limit, (end - limit)
    r_moe = r1 + 31744
    XT_END, HT_END = r_xt + 2 * XW * 4, r1

    x_hi, x_lo = lay(r_xt, XT_END, ("x_hi", [P, XW], F32R), ("x_lo", [P, XW], F32R))
    (ht,) = lay(r_ht, HT_END, ("ht", [P, KT, N], F32))
    (xn,) = lay(r1, end, ("xn", [P, NT, DM], F32))
    li, lf, bcum, g_r, m_r, mt, nm, em = lay(r_ht, HT_END, *[(f"row_{n}", [H, N], F32) for n in
                                             ("li", "lf", "b", "g", "m", "mt", "nm", "em")])
    w_r = lf
    (qt, kt, ve, kw, kwm, pb, ps_, cb, cp, hh, bm, smk, qm) = lay(
        r1, end, ("qt", [P, 2, N], F32), ("kt", [P, 2, N], F32), ("ve", [P, NT, VW], F32),
        ("kw", [P, PT, DH], F32), ("kwm", [NS, DB, DH], F32), ("pb", [P, 1280], F32), ("ps_", [NS, NS], F32),
        ("cb", [P, DB, 2, VW], F32), ("cp", [P, 2, VW], F32), ("hh", [P, NT, DH], F32), ("bm", [P, H, N], F32),
        ("smk", [P, H, DB, NS], F32), ("qm", [P, 2, DB, NS], F32))
    assert size([P, NT, DH]) + size([P, H, N]) + size([P, H, DB, NS]) >= 4 * KT * P * 4
    at_hh = r1 + sum(size(x) for x in ([P, 2, N], [P, 2, N], [P, NT, VW], [P, PT, DH], [NS, DB, DH], [P, 1280],
                                       [NS, NS], [P, DB, 2, VW], [P, 2, VW]))
    wg_hi = place("wg_hi", [P, 2, KT, P], F32R, at_hh)
    wg_lo = place("wg_lo", [P, 2, KT, P], F32R, at_hh + 2 * KT * P * 4)
    gh, sg0, sg1, sg2, sg3, wp, spn = lay(
        r1, r_moe, ("gh", [P, KT, N], F32R), ("sg0", [P, N], F32), ("sg1", [P, N], F32), ("sg2", [P, N], F32),
        ("sg3", [P, N], F32), ("wp", [P, NG, GD], F32), ("spn", [DB * BUF, NG * GD], F32))
    sg = [sg0, sg1, sg2, sg3]
    (gl,) = lay(r_ht, HT_END, ("gl", [P, KT, N], F32R))
    po = place("po", [P, NG, (DB + 1) * BUF], F32, r1 + (KT + 2) * N * 4)
    pool_p = place("pool_p", [BUF, NG * GD], F32, r1 + (KT + 3) * N * 4)
    pool_s = place("pool_s", [DB * BUF, NG * GD], F32, r1 + (KT + 4) * N * 4 + NG * GD * 4)
    r_pool = r_moe
    r_mx = r_pool + 19584
    ext, pt = lay(r_pool, r_mx, ("ext", [P, NG, EXT], F32), ("pt", [P, NG, N], F32))
    sa, sbb = lay(r_mx, end, ("sa", [P, NG, EXT], F32), ("sbb", [P, NG, EXT], F32))
    pbh = place("pbh", [P, NG, N], F32R, r_mx)
    pbl = place("pbl", [P, NG, N], F32R, r_mx + size([P, NG, EXT]))
    (yb,) = lay(r_pool, r_mx, ("yb", [P, KT, N], F32))
    (mxl,) = lay(r_pool, r_mx, ("mxl", [P, XW], F32R))
    (mxh,) = lay(r_mx, end, ("mxh", [P, XW], F32R))
    x1, lng, lnb = lay(r_xt, XT_END, ("x1", [P, NT, DM], F32), ("lng", [P, DM], F32), ("lnb", [P, DM], F32))
    after_ln = r_xt + NT * DM * 4 + 2 * DM * 4
    hth, htl = lay(after_ln, XT_END, ("hth", [P, 4, P], F32R), ("htl", [P, 4, P], F32R))
    raw2 = place("raw2", [P, MOE_SLOTS, CHUNK], F32, r_ht)
    assert r_ht + MOE_SLOTS * CHUNK * 4 <= r_moe
    x1t, onehot = lay(r_moe, end, ("x1t", [P, KT, N], F32), ("onehot", [P, NT, NE, P], BF16))
    rt = lay(r_moe + size([P, KT, N]) + NT * NE * P * 2, end, *[(f"rt{i}", [P, NT, NE], F32) for i in range(9)])
    lg, pr, rk, tmp_r, sel, gate, s1, pos, dest = rt
    (rsm,) = lay(after_ln, XT_END, ("rsm", [P, 6, NT * EG], F32))
    gates_ab, dest_f, dx, cnt_v, ovf, incl, obase, zero16, idx_f, ovx, tok_bf, dest_i, idx_i, idx_c, ctl = lay(
        after_ln + 2 * size([P, 4, P]), XT_END, ("gates_ab", [P, 2, NT], F32), ("dest_f", [P, 2, NT], F32),
        ("dx", [P, 2, NT], F32), ("cnt_v", [P, NE], F32), ("ovf", [P, NE], F32), ("incl", [P, NE], F32),
        ("obase", [P, NE], F32), ("zero16", [P, NE], F32), ("idx_f", [P, 2 * NE], F32), ("ovx", [P, XTRA, NE], F32),
        ("tok_bf", [P, NT * 2], BF16), ("dest_i", [P, 2, NT], I32), ("idx_i", [P, NE], I32), ("idx_c", [P, 1], I32),
        ("ctl", [P, XTRA + 1], I32))
    xg, xgh, xgl, gs, hs, ys, oh2 = lay(
        r_moe, end, ("xg", [P, DM], F32), ("xgh", [P, KT, P], F32R), ("xgl", [P, KT, P], F32R),
        ("gs", [P, DE], F32), ("hs", [P, DE], F32), ("ys", [P, DM], F32), ("oh2", [P, 2, NT, P], BF16))
    ya, ybk = lay(r_moe, end, ("ya", [P, NT, DM], F32), ("ybk", [P, NT, DM], F32))

    psum = ctx.enter_context(nc.psum_tensor("psum", [P, 8, 512], F32))

    def wide(j):
        return psum[:, 2 * (j % 2):2 * (j % 2) + 2, :]

    def narrow(j):
        return psum[:, 4 + j % 2, :]

    def third(j):
        return psum[:, 6 + j % 2, :]

    def halves(j):
        return wide(j)[:, :, 0:HALF]

    cst_in, par_in, gate_in, wg_in, nn_in, spn_in, wp_in, x1in, ln_in, wr_in = (
        sem(n) for n in (
            "cst_in", "par_in", "gate_in", "wg_in", "nn_in", "spn_in", "wp_in", "x1in", "ln_in", "wr_in"))
    x_in = [sem(f"x_in{i}") for i in range(NT)]
    raw_in = [sem(f"raw_in{i}") for i in range(RAW_SLOTS)]
    raw2_in = [sem(f"raw2_in{i}") for i in range(MOE_SLOTS)]
    c_in, c_out, cp_out, outs, m_out, n_out, pool_out = (
        sem(n) for n in ("c_in", "c_out", "cp_out", "outs", "m_out", "n_out", "pool_out"))
    w_hi, w_lo = sem("w_hi"), sem("w_lo")
    z_done, t_done, h_done = sem("z_done"), sem("t_done"), sem("h_done")
    z_free = [sem("z_free0"), sem("z_free1")]
    t_free = [sem("t_free0"), sem("t_free1")]
    h_free = [sem("h_free0"), sem("h_free1")]
    x_hi_ok, wgh_ok, wgl_ok, wgz_ok = (sem(n) for n in ("x_hi_ok", "wgh_ok", "wgl_ok", "wgz_ok"))
    dve, act, pool = sem("dve_step"), sem("act_step"), sem("pool_step")
    gate_m, gate_l, row_ok, em_ok, rows_dve = (
        sem(n) for n in ("gate_m", "gate_l", "row_ok", "em_ok", "rows_dve"))
    ready = sem("ready")
    diag_ok, e_ok, n_ok, qm_ok, var_ok, rstd_ok, hn_ok, c_upd, cp_ok, = (
        sem(n) for n in ("diag_ok", "e_ok", "n_ok", "qm_ok", "var_ok", "rstd_ok", "hn_ok", "c_upd", "cp_ok",
                         ))
    pt_ok, po_ok, pbh_ok, hg_ok, gh_ok, gl_ok, = (
        sem(n) for n in ("pt_ok", "po_ok", "pbh_ok", "hg_ok", "gh_ok",
                         "gl_ok", ))
    mt2_ok, mix_ok, mxh_ok, mxl_ok = (
        sem(n) for n in ("mt2_ok", "mix_ok", "mxh_ok", "mxl_ok"))
    lv_ok, lr_ok, lc_ok, ln_ok, lg_ok, x1_out, x1_ok = (
        sem(n) for n in ("lv_ok", "lr_ok", "lc_ok", "ln_ok", "lg_ok", "x1_out", "x1_ok"))
    sh_ok, se_ok, sel_ok, oh_ok, idx_ok, xa_ok = (
        sem(n) for n in ("sh_ok", "se_ok", "sel_ok", "oh_ok", "idx_ok", "xa_ok"))
    g_in, xt_done, xgh_ok, xgl_ok, w_used, sig_ok, hs_ok, hi_done, hth_ok, htl_ok, ya_ok, yd_ok, y_out = (
        sem(n) for n in ("g_in", "xt_done", "xgh_ok", "xgl_ok", "w_used", "sig_ok", "hs_ok", "hi_done", "hth_ok",
                         "htl_ok", "ya_ok", "yd_ok", "y_out"))
    oh2_ok, ix2_done, ix2_ok, held_ok = (sem(n) for n in ("oh2_ok", "ix2_done", "ix2_ok", "held_ok"))
    yg_in = [sem(f"yg_in{i}") for i in range(NT)]
    idc_ok, xal_ok, dve_tail = sem("idc_ok"), sem("xal_ok"), sem("dve_tail")
    fin_ok, v2_ok, r2_ok, c2_ok, n2_ok, g2_ok = (sem(n) for n in ("fin_ok", "v2_ok", "r2_ok", "c2_ok", "n2_ok", "g2_ok"))

    def z_room(eng, j, more=0):
        eng.wait_ge(z_free[j % 2], more + j // 2)

    def z_evacuated(eng, j, more=0):
        eng.wait_ge(z_free[j % 2], more + (j // 2 + 1))

    def t_room(eng, j, more=0):
        eng.wait_ge(t_free[j % 2], more + j // 2)

    def h_room(eng, j, more=0):
        eng.wait_ge(h_free[j % 2], more + (j // 2 + 1))

    def h_evac(eng, j, more=0):
        eng.wait_ge(h_free[j % 2], more + (j // 2 + 2))

    def t_evacuated(eng, j, more=0):
        eng.wait_ge(t_free[j % 2], more + (j // 2 + 1))

    def chunk_end(c):
        if c < C_O:
            return J_HEAD + PER_HEAD * (c // 3) + 2 * (c % 3) + 1
        if c < C_PB:
            return J_O + 2 * (c - C_O) + 1
        if c < C_MIX:
            return J_PB + 4 * (c - C_PB) + 3
        if c < C_WO:
            return J_MIX + PER_MIX * ((c - C_MIX) // 3) + 2 * ((c - C_MIX) % 3) + 1
        return J_WO + 2 * (c - C_WO) + 1

    def dense_split_hi(eng, c, turn=0, per=0):
        eng.wait_ge(raw_in[c % RAW_SLOTS], 16 * turn + 16 * (c // RAW_SLOTS + 1))
        if c >= SPLIT_SLOTS:
            eng.wait_ge(z_done, per * turn + (chunk_end(c - SPLIT_SLOTS) + 1))
        nc.scalar.copy(split_hi[:, c % SPLIT_SLOTS, :], raw[:, c % RAW_SLOTS, :]).then_inc(w_hi, 1)

    def dense_split_lo(eng, c, turn=0):
        eng.wait_ge(w_hi, 3 * turn + (c + 1))
        slot = c % SPLIT_SLOTS
        nc.vector.tensor_tensor(split_lo[:, slot, :], raw[:, c % RAW_SLOTS, :], split_hi[:, slot, :].bitcast(F32),
                                ALU.subtract).then_inc(w_lo, 1)

    def product3(out, a_hi, a_lo, b_hi, b_lo, first, last):
        nc.tensor.matmul(out, a_lo, b_hi, start=first, stop=False)
        nc.tensor.matmul(out, a_hi, b_lo, start=False, stop=False)
        return nc.tensor.matmul(out, a_hi, b_hi, start=False, stop=last)

    def xcols(t, k, a, n):
        return t[:, k * N + a:k * N + a + n]

    whole = lambda c: slice(c * P, (c + 1) * P)
    PB_AT = [0, 512, 896, 1152]

    block = ctx.enter_context(nc.Block())

    @block.sync
    def _(sp):
        def load_chunk(c, src, more=0, k=KT):
            s = c % RAW_SLOTS
            if c >= RAW_SLOTS:
                sp.wait_ge(w_lo, more + (c - RAW_SLOTS + 1))
            dst = raw[:, s, :].rearrange("p (k n) -> p k n", k=k)
            sp.dma_start(dst, src).then_inc(raw_in[s], 16)

        def win(col_, n=256):
            return w_in[0][:, col_:col_ + n].rearrange("(k p) n -> p k n", p=P)

        def head_cols(first, h):
            return w_in[0].rearrange("(k p) n -> p k n", p=P)[:, :, bass.ds(first + h * DH, DH)]

        sp.dma_start(cst[:], consts).then_inc(cst_in, 16)
        for i in range(PT):
            sp.dma_start(xn[:, i, :], x_prompt[0, i * P:(i + 1) * P, :]).then_inc(x_in[i], 16)
        sp.dma_start(xn[0:NS, PT, :], x_sample.rearrange("b t d -> (b t) d")).then_inc(x_in[PT], 16)
        gcol = 4 * DM
        with nc.allow_non_contiguous_dma(reason="eight gate columns and small parameters"):
            sp.dma_start(wg_raw[:], w_in[0][:, gcol:gcol + 8].rearrange("(k p) n -> p k n", p=P)).then_inc(wg_in, 16)
            sp.dma_start(bias_g[:], b_gate[0].rearrange("(q h) -> h q", q=2)).then_inc(gate_in, 16)
            sp.dma_start(m_prev[:], state_m[0].rearrange("b h -> h b")).then_inc(gate_in, 16)
            load_chunk(0, win(0))
            load_chunk(1, win(DM))
            load_chunk(2, win(2 * DM))
            sp.dma_start(gain[:], hn_gain[0].rearrange("h (c p) -> p (h c)", p=P)).then_inc(par_in, 16)
            sp.dma_start(pscale[:], pool_scale[0].rearrange("(g p) -> p g", p=P)).then_inc(par_in, 16)
            sp.dma_start(brt[:], b_router.partition_broadcast(P)).then_inc(par_in, 16)
            sp.dma_start(wr[:], w_router.rearrange("(k p) n -> p k n", p=P)).then_inc(wr_in, 16)
            sp.dma_start(nn[:], state_n[0].rearrange("b h d -> (b h) d")).then_inc(nn_in, 16)

        def head_state(h):
            return [state_C[0][:, bass.ds(h, 1), dt * P:(dt + 1) * P, :].rearrange("b o p e -> p (b o) e")
                    for dt in range(2)]

        for dt in range(2):
            sp.dma_start(cb[:, :, dt, 0:DH], state_C[0][:, 0, dt * P:(dt + 1) * P, :].rearrange("b p e -> p b e")
                         ).then_inc(c_in, 16)

        def next_head(h, more):
            for j in range(3):
                s = (3 + j) % RAW_SLOTS
                sp.wait_ge(w_lo, more + (j + 1))
                dst = raw[:, s, :].rearrange("p (k n) -> p k n", k=KT)
                sp.dma_start(dst, head_cols(j * DM + DH, h)).then_inc(raw_in[s], 16)

        def store_state(h):
            sp.wait_ge(cp_ok, h + 1)
            sp.dma_start(C_prompt[0, 0][bass.ds(h, 1)].rearrange("o (t p) e -> p (o t) e", p=P),
                         cp[:, :, 0:DH]).then_inc(cp_out, 16)
            sp.wait_ge(c_upd, h + 1)
            for dt in range(2):
                sp.dma_start(C_sample[0][:, bass.ds(h, 1), dt * P:(dt + 1) * P, :].rearrange("b o p e -> p (b o) e"),
                             cb[:, :, dt, 0:DH]).then_inc(c_out, 16)

        with sp.Fori(0, H - 1) as h:
            next_head(h, 3 * h)
            store_state(h)
            sp.wait_ge(c_out, 32 * h + 32)
            for dt, src in enumerate(head_state(h + 1)):
                sp.dma_start(cb[:, :, dt, 0:DH], src).then_inc(c_in, 16)
        u0 = 4 * DM + 2 * H
        load_chunk(C_O, win(3 * DM))
        load_chunk(C_O + 1, win(3 * DM + 256))
        load_chunk(C_U, win(u0))
        store_state(H - 1)
        sp.wait_ge(z_done, J_O)
        sp.dma_start(spn[:], state_pool[0].rearrange("b j c -> (b j) c")).then_inc(spn_in, 16)
        sp.dma_start(wp[:], w_pool[0].rearrange("g c e -> c g e")).then_inc(wp_in, 16)
        with nc.allow_non_contiguous_dma(reason="one number for each head and sequence"):
            sp.wait_ge(rows_dve, 1)
            sp.dma_start(m_prompt[0].rearrange("o h -> h o"), mout[:, DB:DB + 1]).then_inc(m_out, 16)
            sp.dma_start(m_sample[0].rearrange("b h -> h b"), mout[:, 0:DB]).then_inc(m_out, 16)
        load_chunk(C_U + 1, win(u0 + 256))
        for j in range(2):
            load_chunk(C_O2 + j, win(3 * DM + 512 + 256 * j))
        for j in range(2):
            load_chunk(C_PB + j, w_proj_b[0][:, 512 * j:512 * j + 512].rearrange("(k p) n -> p k n", p=P), k=4)
        g0 = u0 + NG * GD
        w_a = w_proj_a[0].rearrange("(k p) n -> p k n", p=P)
        for j in range(3):
            load_chunk(C_MIX + j, [win(g0), win(g0 + DM), w_a[:, :, 0:256]][j])
        t_evacuated(sp, T_POUT)
        sp.dma_start(pool_prompt[0, 0], pool_p[:]).then_inc(pool_out, 16)
        sp.dma_start(pool_sample[0].rearrange("b j c -> (b j) c"), pool_s[:]).then_inc(pool_out, 16)
        t_evacuated(sp, T_NOUT)
        for dt in range(2):
            sp.dma_start(n_prompt[0, 0][:, dt * P:(dt + 1) * P], nrows[4 * dt:4 * dt + 4, :]).then_inc(n_out, 16)
            sp.dma_start(n_sample[0][:, :, dt * P:(dt + 1) * P].rearrange("b h d -> (b h) d"),
                         nrows[8 + 32 * dt:40 + 32 * dt, :]).then_inc(n_out, 16)
        w_all = w_in[0].rearrange("(k p) n -> p k n", p=P)
        with sp.Fori(0, 3) as t:
            for j in range(3):
                c = C_MIX + 3 + j
                s = c % RAW_SLOTS
                sp.wait_ge(w_lo, 3 * t + (c - RAW_SLOTS + 1))
                dst = raw[:, s, :].rearrange("p (k n) -> p k n", k=KT)
                src = (w_all[:, :, bass.ds(g0 + 256 + t * 256, 256)], w_all[:, :, bass.ds(g0 + DM + 256 + t * 256, 256)],
                       w_a[:, :, bass.ds(256 + t * 256, 256)])[j]
                sp.dma_start(dst, src).then_inc(raw_in[s], 16)
        w_o = w_out[0].rearrange("(k p) n -> p k n", p=P)
        for j in range(4):
            load_chunk(C_WO + j, w_o[:, :, 256 * j:256 * j + 256])
        sp.wait_ge(z_done, J_WO)
        sp.wait_ge(y_out, 32)
        for i in range(PT):
            sp.dma_start(x1[:, i, :], x_prompt[0, i * P:(i + 1) * P, :]).then_inc(x1in, 16)
        sp.dma_start(x1[0:NS, PT, :], x_sample.rearrange("b t d -> (b t) d")).then_inc(x1in, 16)
        sp.dma_start(lng[:], ln1_g[0].partition_broadcast(P)).then_inc(ln_in, 16)
        sp.dma_start(lnb[:], ln1_b[0].partition_broadcast(P)).then_inc(ln_in, 16)

        def expert_chunk(slot, n_wait, wt, e, half):
            if n_wait is not None:
                sp.wait_ge(w_lo, n_wait)
            dst = raw2[:, slot, :].rearrange("p (k n) -> p k n", k=4)
            if wt is w_e_down:
                src = wt[0][bass.ds(e, 1)].rearrange("o (k p) n -> p (o k) n", p=P)[:, :, half * 512:half * 512 + 512]
            else:
                src = wt[0][bass.ds(e, 1), half * 512:half * 512 + 512, :].rearrange("o (k p) n -> p (o k) n", p=P)
            sp.dma_start(dst, src).then_inc(raw2_in[slot], 16)

        sp.wait_ge(mxl_ok, KT)
        sp.wait_ge(pool_out, 32)
        for n, (wt, half) in enumerate(((w_e_gate, 0), (w_e_gate, 1), (w_e_up, 0), (w_e_up, 1))):
            expert_chunk(n, None, wt, 0, half)

        def store_rows():
            for i in range(NT):
                sp.wait_ge(x1_ok, i + 1)
                r = ROWS[i]
                sp.dma_start(x1_rows[i * P:i * P + r, :], x1[0:r, i, :]).then_inc(x1_out, 16)

        store_rows()
        sp.wait_ge(x1_out, 16 * NT)
        sp.wait_ge(lc_ok, NT)
        sp.dma_start(lng[:], ln2_g[0].partition_broadcast(P)).then_inc(ln_in, 16)
        sp.dma_start(lnb[:], ln2_b[0].partition_broadcast(P)).then_inc(ln_in, 16)
        with sp.Fori(1, NE) as e:
            for j, (wt, half) in enumerate(((w_e_gate, 0), (w_e_gate, 1), (w_e_up, 0), (w_e_up, 1),
                                            (w_e_down, 0), (w_e_down, 1))):
                n = 4 + j
                expert_chunk(n % MOE_SLOTS, 6 * e + (C_MOE + n - 6 + 1 - 6), wt, e if j < 4 else e - 1, half)
        for j in range(2):
            n = 94 + j
            expert_chunk(n % MOE_SLOTS, C_MOE + n - 6 + 1, w_e_down, NE - 1, j)
        sp.wait_ge(xa_ok, 1)
        extra = sp.value_load(ctl[0:1, XTRA:XTRA + 1], min_val=0, max_val=XTRA)
        with sp.Fori(0, XTRA) as j:
            with sp.If(extra > j):
                e = sp.value_load(ctl[0:1, bass.ds(j, 1)], min_val=0, max_val=NE - 1)
                for m, (wt, half) in enumerate(((w_e_gate, 0), (w_e_gate, 1), (w_e_up, 0), (w_e_up, 1),
                                                (w_e_down, 0), (w_e_down, 1))):
                    expert_chunk(m, 6 * j + (C_MOE + 96 + m - 6 + 1), wt, e, half)
            sp.nop()
        for i in range(NT):
            r = ROWS[i]
            sp.wait_ge(fin_ok, i + 1)
            dst = y_prompt[0, i * P:(i + 1) * P, :] if i < PT else y_sample.rearrange("b t d -> (b t) d")
            sp.dma_start(dst, x1[0:r, i, :]).then_inc(outs, 16)
        sp.wait_ge(outs, 16 * NT)
        sp.wait_ge(pool_out, 32)
        sp.wait_ge(n_out, 64)
        sp.wait_ge(m_out, 32)
        sp.wait_ge(c_out, 32 * H)
        sp.wait_ge(cp_out, 16 * H)

    @block.gpsimd
    def _(pl):
        minus_half = const("half")

        pl.wait_ge(cst_in, 16)
        pl.wait_ge(ready, H)
        for b in range(0, XTRA, 4):
            pl.dma_start(y_slots[(NE + b) * P:(NE + b + 4) * P, :].rearrange("(b p) d -> p b d", p=P),
                         x_hi[:, 0:4 * DM].bitcast(F32).rearrange("p (b d) -> p b d", b=4)).then_inc(y_out, 16)
        with pl.Fori(0, H) as h:
            pl.wait_ge(var_ok, h + 1)
            nc.gpsimd.tensor_tensor(hrs[:], hve[:], minus_half, ALU.pow).then_inc(rstd_ok, 1)
        with pl.Fori(0, 4) as t:
            for c in range(2):
                z_evacuated(pl, J_MIX + 2 + c, 3 * t)
                ybt = yb[:, bass.ds(2 * t + c, 1), :].rearrange("p o n -> p (o n)")
                nc.gpsimd.tensor_tensor(sg[2 + c][:], sg[2 + c][:], ybt, ALU.mult).then_inc(mt2_ok, 1)
        for i in range(NT + 1):
            if i < NT:
                r = ROWS[i]
                pl.wait_ge(lv_ok, i + 1)
                nc.gpsimd.tensor_tensor(hrs[0:r, i:i + 1], hve[0:r, i:i + 1], minus_half[0:r, 0:1],
                                        ALU.pow).then_inc(lr_ok, 1)
            if i == 1:
                pl.wait_ge(ln_in, 32)
            if i:
                r = ROWS[i - 1]
                pl.wait_ge(ln_ok, i)
                nc.gpsimd.tensor_tensor(x1[0:r, i - 1, :], x1[0:r, i - 1, :], lng[0:r, :], ALU.mult).then_inc(lg_ok, 1)

        def hold():
            nc.gpsimd.tensor_tensor(held[:], minus_half[0:1, 0:1], minus_half[0:1, 0:1], ALU.add
                                    ).then_inc(held_ok, 1)

        def gather():
            idx = bass.IndirectOffsetOnAxis(ap=idx_c[:].bitcast(U32), axis=0)
            pl.indirect_dma_start(xg[:], None, x1_rows, idx).then_inc(g_in, 16)

        pl.wait_ge(idx_ok, 1)
        nc.gpsimd.tensor_copy(idx_c[:], idx_i[:, 0:1]).then_inc(idc_ok, 1)
        pl.wait_ge(x1_out, 16 * NT)
        pl.wait_ge(idc_ok, 1)
        gather()
        pl.wait_ge(xt_done, 1)
        nc.gpsimd.tensor_copy(idx_c[:], idx_i[:, 1:2]).then_inc(idc_ok, 1)
        pl.wait_ge(idc_ok, 2)
        gather()
        pl.wait_ge(y_out, 32)
        with pl.Fori(1, NE - 1) as e:
            pl.wait_ge(xt_done, e + 1)
            nc.gpsimd.tensor_copy(idx_c[:], idx_i[:, bass.ds(e + 1, 1)]).then_inc(idc_ok, 1)
            pl.wait_ge(idc_ok, e + 2)
            hold()
            gather()
            pl.wait_ge(ya_ok, e)
            pl.wait_ge(yd_ok, e)
            pl.dma_start(y_slots[bass.ds((e - 1) * P, P), :], ys[:]).then_inc(y_out, 16)
        for e in (NE - 2, NE - 1):
            pl.wait_ge(ya_ok, e + 1)
            pl.wait_ge(yd_ok, e + 1)
            pl.dma_start(y_slots[e * P:(e + 1) * P, :], ys[:]).then_inc(y_out, 16)
        pl.wait_ge(y_out, 16 * (NE + 2))
        extra = pl.value_load(ctl[0:1, XTRA:XTRA + 1], min_val=0, max_val=XTRA)
        with pl.Fori(0, XTRA) as j:
            with pl.If(extra > j):
                pl.wait_ge(ix2_ok, j + 1)
                pl.wait_ge(held_ok, j + (NE - 2))
                hold()
                gather()
                pl.wait_ge(ya_ok, j + (NE + 1))
                pl.wait_ge(yd_ok, j + (NE + 1))
                pl.dma_start(y_slots[bass.ds((j + NE) * P, P), :], ys[:]).then_inc(y_out, 16)
                pl.wait_ge(y_out, 16 * j + 16 * (NE + 3))
            pl.nop()
        for i in range(NT):
            r = ROWS[i]
            for a, buf in enumerate((ya, ybk)):
                idx = bass.IndirectOffsetOnAxis(ap=dest_i[0:r, a, i:i + 1].bitcast(U32), axis=0)
                pl.indirect_dma_start(buf[0:r, i, :], None, y_slots, idx).then_inc(yg_in[i], 16)
        pl.wait_ge(ln_in, 64)
        for i in range(NT + 1):
            if i < NT:
                r = ROWS[i]
                pl.wait_ge(v2_ok, i + 1)
                nc.gpsimd.tensor_tensor(hrs[0:r, i:i + 1], hve[0:r, i:i + 1], minus_half[0:r, 0:1],
                                        ALU.pow).then_inc(r2_ok, 1)
            if i:
                r = ROWS[i - 1]
                pl.wait_ge(n2_ok, i)
                nc.gpsimd.tensor_tensor(x1[0:r, i - 1, :], x1[0:r, i - 1, :], lng[0:r, :], ALU.mult).then_inc(g2_ok, 1)

    @block.scalar
    def _(ac):
        st = Steps(act)
        for i in range(NT):
            r = ROWS[i]
            ac.wait_ge(z_done, J_X + i + 1)
            src = wide(J_X + i).rearrange("p b (q t) -> p (b q) t", q=4)[:, :, 0:r]
            nc.scalar.copy(x_hi[:, 0:KT * N].rearrange("p (k t) -> p k t", k=KT)[:, :, i * P:i * P + r],
                           src).then_inc(x_hi_ok, 1)
        ac.wait_ge(wg_in, 16)
        ac.wait_ge(wgz_ok, 1)
        for q in range(2):
            last = nc.scalar.copy(wg_hi[:, q, :, 0:H], wg_raw[:, :, q * H:(q + 1) * H])
        last.then_inc(wgh_ok, 1)
        ac.wait_ge(gate_m, 1)
        nc.scalar.activation(g_r[:], m_r[:], ACT.Exp).then_inc(act, 1)
        ac.wait_ge(act, 1)
        nc.scalar.activation(m_r[:], g_r[:], ACT.Ln, bias=1.0).then_inc(gate_l, 1)
        dense_split_hi(ac, 0)
        ac.wait_ge(row_ok, 1)
        nc.scalar.activation(em[:], mt[:], ACT.Exp, scale=-1.0).then_inc(em_ok, 1)
        nc.scalar.activation(w_r[:], w_r[:], ACT.Exp).then_inc(em_ok, 1)
        nc.scalar.activation(sil[:], sil[:], ACT.Exp).then_inc(em_ok, 1)
        for c in range(1, SPLIT_SLOTS):
            dense_split_hi(ac, c)
        for h in range(H):
            j = J_BM + h
            ac.wait_ge(z_done, j + 1)
            nc.scalar.copy(bm[:, h, :].rearrange("p (a n) -> p a n", a=2), halves(j)).then_inc(z_free[j % 2], 1)

        with ac.Fori(0, H) as h:
            z0, tz = J_HEAD, PER_HEAD * h
            for c in range(2):
                ac.wait_ge(z_done, tz + (z0 + c + 1))
                nc.scalar.copy(qt[:, c, :].rearrange("p (a n) -> p a n", a=2), halves(z0 + c)
                               ).then_inc(z_free[(z0 + c) % 2], 1)
            dense_split_hi(ac, 3, h, PER_HEAD)
            for c in range(2):
                ac.wait_ge(z_done, tz + (z0 + 2 + c + 1))
                nc.scalar.activation(kt[:, c, :].rearrange("p (a n) -> p a n", a=2), halves(z0 + 2 + c), ACT.Copy,
                                     scale=DH ** -0.5).then_inc(z_free[(z0 + 2 + c) % 2], 1)
            dense_split_hi(ac, 4, h, PER_HEAD)
            ac.wait_ge(diag_ok, h + 1)
            for i in range(PT):
                d = pb[:, PB_AT[i]:PB_AT[i] + P]
                nc.scalar.activation(d, d, ACT.Exp)
                if i < PT - 1:
                    w = SEQ - (i + 1) * P
                    src = bm[:, bass.ds(h, 1), (i + 1) * P:SEQ].rearrange("p o n -> p (o n)")
                    nc.scalar.activation(pb[:, PB_AT[i] + P:PB_AT[i] + P + w], src, ACT.Exp, bias=ch[:, i:i + 1])
            nc.scalar.activation(ps_[:], ps_[:], ACT.Exp).then_inc(e_ok, 1)
            dense_split_hi(ac, 5, h, PER_HEAD)
            for dt in range(2):
                ac.wait_ge(h_done, H_PER_HEAD * h + (dt + 1))
                nc.scalar.copy(cp[:, dt, :], third(dt)[:, 0:VW]).then_inc(h_free[dt], 1)
            for c in range(2):
                j = z0 + 6 + c
                ac.wait_ge(z_done, tz + (j + 1))
                dst = ht[:, bass.ds(2 * h + c, 1), :].rearrange("p o n -> p (o n)")
                nc.scalar.activation(dst[:, 0:SEQ], wide(j)[:, 0, :], ACT.Copy, scale=ch[:, 15 + c:16 + c])
                nc.scalar.activation(dst[:, SEQ:N], wide(j)[:, 1, 0:NS], ACT.Copy,
                                     scale=ch[:, 15 + c:16 + c]).then_inc(z_free[j % 2], 1)
            ac.wait_ge(cp_out, 16 * h + 16)

        def output_gates(first, j0):
            for q in range(4):
                ct, j = first + q, j0 + q
                ac.wait_ge(z_done, j + 1)
                if ct >= 2:
                    ac.wait_ge(gl_ok, ct - 1)
                nc.scalar.activation(sg[ct % 2][:].rearrange("p (a n) -> p a n", a=2), halves(j), ACT.Sigmoid
                                     ).then_inc(z_free[j % 2], 1)
                if q % 2:
                    dense_split_hi(ac, (C_O, C_O2)[first // 4] + q // 2 + 3)
                ac.wait_ge(hg_ok, ct + 1)
                nc.scalar.copy(gh[:, ct, :], sg[ct % 2][:]).then_inc(gh_ok, 1)

        output_gates(0, J_O)
        ac.wait_ge(c_out, 32 * H)
        ac.wait_ge(cp_out, 16 * H)
        for g in range(NG):
            j = J_U + g
            ac.wait_ge(z_done, j + 1)
            nc.scalar.copy(ext[:, g, BUF:BUF + HALF], wide(j)[:, 0, 0:HALF])
            nc.scalar.copy(ext[:, g, BUF + HALF:BUF + SEQ], wide(j)[:, 1, 0:SEQ - HALF])
            v = ext[:, g, BUF + SEQ:EXT].rearrange("p (b t) -> p b t", b=DB)[:, :, BUF:BUF + DT]
            nc.scalar.copy(v, wide(j)[:, 1, SEQ - HALF:HALF].rearrange("p (b t) -> p b t", b=DB)
                           ).then_inc(z_free[j % 2], 1)
            if g % 2:
                dense_split_hi(ac, C_U + g // 2 + 3)
        output_gates(4, J_O2)
        for g in range(NG):
            j = J_WP + g
            ac.wait_ge(z_done, j + 1)
            nc.scalar.activation(pbh[:, g, :].rearrange("p (a n) -> p a n", a=2), halves(j), ACT.Copy,
                                 scale=pscale[:, g:g + 1]).then_inc(pbh_ok, 1)
        for ct in range(KT):
            j = J_PB + ct
            ac.wait_ge(z_done, j + 1)
            nc.scalar.copy(yb[:, ct, :].rearrange("p (a n) -> p a n", a=2), halves(j)).then_inc(z_free[j % 2], 1)
            if ct % 4 == 3:
                dense_split_hi(ac, C_PB + ct // 4 + 3)
        ac.wait_ge(pool_out, 32)
        with ac.Fori(0, 4) as t:
            tz = PER_MIX * t
            for q in range(4):
                j = J_MIX + q
                ac.wait_ge(z_done, tz + (j + 1))
                nc.scalar.activation(sg[q][:].rearrange("p (a n) -> p a n", a=2), halves(j), ACT.Sigmoid
                                     ).then_inc(z_free[j % 2], 1)
                if q % 2:
                    dense_split_hi(ac, C_MIX + 3 + q // 2, t, PER_MIX)
            for c in range(2):
                ac.wait_ge(mix_ok, 2 * t + (c + 1))
                nc.scalar.copy(mxh[:, bass.ds((2 * t + c) * N, N)], sg[c][:]).then_inc(mxh_ok, 1)
            dense_split_hi(ac, C_MIX + 5, t, PER_MIX)
            ac.wait_ge(mxl_ok, 2 * t + 2)
        dense_split_hi(ac, C_WO + 3)

        def expert_hi(n, used_sem, used, in_more=0):
            ac.wait_ge(raw2_in[n % MOE_SLOTS], in_more + 16 * (n // MOE_SLOTS + 1))
            ac.wait_ge(used_sem, used)
            nc.scalar.copy(split_hi[:, (C_MOE + n) % SPLIT_SLOTS, :], raw2[:, n % MOE_SLOTS, :]).then_inc(w_hi, 1)

        for n in range(3):
            expert_hi(n, z_done, chunk_end(C_MOE + n - 3) + 1)

        def evac_x1t(i):
            ac.wait_ge(z_done, J_XT + i + 1)
            r = ROWS[i]
            src = wide(J_XT + i).rearrange("p b (q t) -> p (b q) t", q=4)[:, :, 0:r]
            nc.scalar.copy(x1t[:, :, i * P:i * P + r], src).then_inc(z_free[(J_XT + i) % 2], 1)

        for i in range(NT):
            r = ROWS[i]
            ac.wait_ge(lc_ok, i + 1)
            nc.scalar.activation(x1[0:r, i, :], x1[0:r, i, :], ACT.Identity, scale=hrs[0:r, i:i + 1],
                                 bias=hnm[0:r, i:i + 1]).then_inc(ln_ok, 1)
            if i >= 2:
                evac_x1t(i - 2)
        evac_x1t(NT - 2)
        evac_x1t(NT - 1)
        ac.wait_ge(sh_ok, 1)
        nc.scalar.activation(pr[:], lg[:], ACT.Exp).then_inc(se_ok, 1)
        ac.wait_ge(x1_out, 16 * NT)
        for i in range(NT):
            r = ROWS[i]
            nc.scalar.mul(x1[0:r, i, :], x1[0:r, i, :], ALPHA).then_inc(xal_ok, 1)

        def split_x():
            nc.scalar.copy(xgh[:], wide(0).rearrange("p b (q t) -> p (b q) t", q=4)).then_inc(xgh_ok, 1)

        def split_h():
            nc.scalar.copy(hth[:], psum[:, 6, :].rearrange("p (q t) -> p q t", q=4)).then_inc(hth_ok, 1)

        def gate_sigmoid():
            nc.scalar.activation(gs[:], psum[:, 2, :], ACT.Sigmoid).then_inc(sig_ok, 1)

        def store_half():
            nc.scalar.copy(ys[:, 0:512], psum[:, 4, :]).then_inc(ya_ok, 1)

        ac.wait_ge(xt_done, 1)
        split_x()
        for n in range(4):
            if n == 2:
                gate_sigmoid()
            expert_hi(n + 3, w_used, n + 1)
        ac.wait_ge(xt_done, 2)
        split_x()
        ac.wait_ge(hi_done, 1)
        split_h()

        def turn(e, last=False):
            for j in range(6):
                if j == 2:
                    ac.wait_ge(hs_ok, e)
                    gate_sigmoid()
                if j == 4 and not last:
                    ac.wait_ge(xt_done, e + 2)
                    split_x()
                if j < 5 or not last:
                    expert_hi(7 + j, w_used, 6 * e + (j - 1), 16 * e - 16)
            ac.wait_ge(w_used, 6 * e + 4)
            ac.wait_ge(y_out, 16 * e + 16)
            store_half()
            ac.wait_ge(hi_done, e + 1)
            split_h()

        with ac.Fori(1, NE - 1) as e:
            turn(e)
        turn(NE - 1, last=True)
        ac.wait_ge(w_used, 6 * NE)
        ac.wait_ge(y_out, 16 * (NE + 1))
        store_half()
        extra = ac.value_load(ctl[0:1, XTRA:XTRA + 1], min_val=0, max_val=XTRA)
        with ac.Fori(0, XTRA) as j:
            with ac.If(extra > j):
                ac.wait_ge(xt_done, j + (NE + 1))
                split_x()
                for m in range(6):
                    expert_hi(m, w_used, 6 * j + (94 + m), 16 * j + 256)
                    if m == 3:
                        ac.wait_ge(w_used, 6 * j + 98)
                        gate_sigmoid()
                ac.wait_ge(hi_done, j + (NE + 1))
                split_h()
                ac.wait_ge(w_used, 6 * j + 102)
                store_half()
            ac.nop()
        for i in range(NT):
            r = ROWS[i]
            ac.wait_ge(c2_ok, i + 1)
            nc.scalar.activation(x1[0:r, i, :], x1[0:r, i, :], ACT.Identity, scale=hrs[0:r, i:i + 1],
                                 bias=hnm[0:r, i:i + 1]).then_inc(n2_ok, 1)

    @block.vector
    def _(ve_):
        v = nc.vector
        st = Steps(dve)

        def step(ins):
            ve_.wait_ge(dve, st.mark(ins))

        def bc(ap, axis, shape):
            return ap.unsqueeze(axis).to_broadcast(shape)

        v.memset(wg_hi[:].bitcast(F32), 0.0)
        v.memset(wg_lo[:].bitcast(F32), 0.0).then_inc(wgz_ok, 1)
        v.memset(x_hi[:, KT * N:].bitcast(F32), 0.0)
        v.memset(x_lo[:, KT * N:].bitcast(F32), 0.0)
        v.memset(col[:], 0.0).then_inc(h_free[0], 1)
        v.memset(hmv[:], 0.0).then_inc(h_free[1], 1)
        v.memset(mt[:, 0:SEQ], 0.0)
        for i in range(NT):
            r = ROWS[i]
            ve_.wait_ge(x_hi_ok, i + 1)
            dst = lambda t: t[:, 0:KT * N].rearrange("p (k t) -> p k t", k=KT)[:, :, i * P:i * P + r]
            src = wide(J_X + i).rearrange("p b (q t) -> p (b q) t", q=4)[:, :, 0:r]
            v.tensor_tensor(dst(x_lo), src, dst(x_hi).bitcast(F32), ALU.subtract).then_inc(z_free[(J_X + i) % 2], 1)
        ve_.wait_ge(wgh_ok, 1)
        for q in range(2):
            last = v.tensor_tensor(wg_lo[:, q, :, 0:H], wg_raw[:, :, q * H:(q + 1) * H],
                                   wg_hi[:, q, :, 0:H].bitcast(F32), ALU.subtract)
        last.then_inc(wgl_ok, 1)
        v.memset(ve[:, :, DH:DH + 1], 1.0)
        v.memset(ve[:, :, DH + 1:VW], 0.0)
        v.memset(cb[:, :, :, DH + 1:VW], 0.0)
        ve_.wait_ge(gate_in, 32)
        for q, (dst, j) in enumerate(((li, J_LI), (lf, J_LF))):
            ve_.wait_ge(z_done, j + 1)
            v.tensor_scalar(dst[:].rearrange("p (a n) -> p a n", a=2), halves(j)[0:H], bias_g[:, q:q + 1], None,
                            ALU.add).then_inc(z_free[j % 2], 1)
        z_evacuated(ve_, J_LI)
        z_evacuated(ve_, J_LF)
        v.scalar_tensor_tensor(m_r[:], lf[:], -1.0, lf[:], ALU.mult, ALU.min).then_inc(gate_m, 1)
        ve_.wait_ge(gate_l, 1)
        step(v.scalar_tensor_tensor(lf[:], lf[:], 0.0, m_r[:], ALU.min, ALU.subtract))
        samp = lambda row: row[:, SEQ:N].rearrange("p (b t) -> p b t", b=DB)
        v.tensor_tensor_scan(bcum[:, 0:SEQ], lf[:, 0:SEQ], mt[:, 0:SEQ], 0.0, ALU.add, ALU.add)
        step(v.tensor_copy(samp(bcum)[:, :, 0:1], samp(lf)[:, :, 0:1]))
        for k in range(1, DT):
            step(v.tensor_tensor(samp(bcum)[:, :, k:k + 1], samp(bcum)[:, :, k - 1:k], samp(lf)[:, :, k:k + 1], ALU.add))
        step(v.tensor_tensor(g_r[:], li[:], bcum[:], ALU.subtract))
        v.tensor_tensor_scan(m_r[:, 0:SEQ], g_r[:, 0:SEQ], g_r[:, 0:SEQ], 0.0, ALU.max, ALU.max)
        mp = m_prev[:].unsqueeze(2)
        step(v.tensor_tensor(samp(m_r)[:, :, 0:1], mp, samp(g_r)[:, :, 0:1], ALU.max))
        for k in range(1, DT):
            step(v.tensor_tensor(samp(m_r)[:, :, k:k + 1], samp(m_r)[:, :, k - 1:k], samp(g_r)[:, :, k:k + 1], ALU.max))
        m_last = samp(m_r)[:, :, DT - 1:DT]
        step(v.tensor_tensor(mt[:], bcum[:], m_r[:], ALU.add))
        v.tensor_copy(mout[:, DB:DB + 1], mt[:, SEQ - 1:SEQ])
        v.tensor_copy(mout[:, 0:DB].unsqueeze(2), samp(mt)[:, :, DT - 1:DT]).then_inc(rows_dve, 1)
        v.tensor_scalar(nm[:], m_r[:], -1.0, None, ALU.mult)
        v.tensor_scalar(w_r[:, 0:SEQ], g_r[:, 0:SEQ], m_r[:, SEQ - 1:SEQ], None, ALU.subtract)
        v.tensor_tensor(samp(w_r), samp(g_r), m_last.to_broadcast([H, DB, DT]), ALU.subtract)
        v.tensor_tensor(sil[:, 0:NS].rearrange("p (b t) -> p b t", b=DB), mp.to_broadcast([H, DB, DT]), samp(m_r),
                        ALU.subtract)
        v.tensor_tensor(sil[:, NS:NS + DB].unsqueeze(2), mp, m_last, ALU.subtract).then_inc(row_ok, 1)
        dense_split_lo(ve_, 0)
        ve_.wait_ge(t_done, T_COL + 1)
        cols = narrow(T_COL)[:, 0:3 * NT * H].rearrange("p (q i h) -> p q i h", q=3, i=NT)
        v.tensor_copy(col[:, :, 0:PT, :], cols[:, :, 0:PT, :])
        v.tensor_copy(col[0:NS, :, PT, :], cols[0:NS, :, PT, :]).then_inc(t_free[T_COL % 2], 1)
        ve_.wait_ge(t_done, T_SIL + 1)
        v.tensor_copy(sb40[:].rearrange("p h n -> p (h n)"), narrow(T_SIL)[:, 0:H * (NS + DB)]
                      ).then_inc(t_free[T_SIL % 2], 1)
        ve_.wait_ge(t_done, T_N + 1)
        v.tensor_copy(ntr[:].rearrange("p c b h -> p (c b h)"), narrow(T_N)[:, 0:2 * NS]).then_inc(t_free[T_N % 2], 1)
        t_evacuated(ve_, T_N)
        t_evacuated(ve_, T_SIL)
        v.tensor_tensor(wm[:], bc(col[0:NS, 2, PT, :], 2, [NS, H, DB]), bc(const("tok_seq", NS), 1, [NS, H, DB]),
                        ALU.mult)
        for h in range(H):
            v.tensor_tensor(smk[:, h], bc(sb40[:, h, 0:NS], 1, [P, DB, NS]),
                            const("seq_of").rearrange("p (b t) -> p b t", b=DB), ALU.mult).then_inc(ready, 1)
        ve_.wait_ge(par_in, 48)
        for c in range(1, SPLIT_SLOTS):
            dense_split_lo(ve_, c)
        ve_.wait_ge(ready, H)

        base = st.base + st.count
        with ve_.Fori(0, H) as h:
            st.loop(h, PER_DVE_HEAD)
            z0, tz, tt, th = J_HEAD, PER_HEAD * h, T_PER_HEAD * h, H_PER_HEAD * h
            z_evacuated(ve_, z0 - 1, 4 * h)
            z_evacuated(ve_, z0 - 2, 4 * h)
            v.tensor_copy(ch[:, 0:15], col[:, :, :, bass.ds(h, 1)].rearrange("p q i o -> p (q i o)"))
            v.tensor_copy(ch[:, 15:17], gain[:, bass.ds(2 * h, 2)])
            step(v.tensor_copy(ch[:, 17:25], sb40[:, bass.ds(h, 1), NS:NS + DB].rearrange("p o b -> p (o b)")))
            row = lambda a, n, r=P: bm[0:r, bass.ds(h, 1), a:a + n].rearrange("p o n -> p (o n)")
            for i in range(PT):
                v.scalar_tensor_tensor(pb[:, PB_AT[i]:PB_AT[i] + P], row(i * P, P), ch[:, i:i + 1], const("causal"),
                                       ALU.add, ALU.add)
            v.scalar_tensor_tensor(ps_[:], row(SEQ, NS, NS), ch[0:NS, PT:PT + 1], const("causal_s", NS),
                                   ALU.add, ALU.add).then_inc(diag_ok, 1)
            ve_.wait_ge(c_in, 32 * h + 32)
            nsrc = ntr[:, :, :, bass.ds(h, 1)].rearrange("p c b o -> p b (c o)")
            v.tensor_copy(cb[:, :, :, DH:DH + 1].rearrange("p b c o -> p b (c o)"), nsrc).then_inc(n_ok, 1)
            dense_split_lo(ve_, 3, h)
            z_evacuated(ve_, z0 + 1, 4 * h)
            for c in range(2):
                last = v.tensor_tensor(qm[:, c], bc(qt[:, c, SEQ:N], 1, [P, DB, NS]),
                                       smk[:, bass.ds(h, 1)].rearrange("p o b t -> p (o b) t"), ALU.mult)
            last.then_inc(qm_ok, 1)
            dense_split_lo(ve_, 4, h)
            ve_.wait_ge(z_done, tz + (z0 + 5))
            v.tensor_copy(ve[:, 0:PT, 0:DH], wide(z0 + 4).rearrange("p b (q n) -> p (b q) n", q=2)
                          ).then_inc(z_free[(z0 + 4) % 2], 1)
            ve_.wait_ge(z_done, tz + (z0 + 6))
            v.tensor_copy(ve[:, PT, 0:DH], wide(z0 + 5)[:, 0, 0:DH]).then_inc(z_free[(z0 + 5) % 2], 1)
            dense_split_lo(ve_, 5, h)
            for q in range(2):
                j = T_HEAD + q
                ve_.wait_ge(t_done, tt + (j + 1))
                for k in range(2):
                    i = 2 * q + k
                    last = v.tensor_scalar(kw[:, i, :], narrow(j)[:, k * DH:(k + 1) * DH], ch[:, 10 + i:11 + i], None,
                                           ALU.mult)
                last.then_inc(t_free[j % 2], 1)
            j = T_HEAD + 2
            ve_.wait_ge(t_done, tt + (j + 1))
            v.tensor_tensor(kwm[:], bc(narrow(j)[0:NS, 0:DH], 1, [NS, DB, DH]),
                            bc(wm[:, bass.ds(h, 1), :].rearrange("p o b -> p (o b)"), 2, [NS, DB, DH]), ALU.mult)
            ve_.wait_ge(e_ok, h + 1)
            v.tensor_tensor(ps_[:], narrow(j)[0:NS, DH:DH + NS], ps_[:], ALU.mult).then_inc(t_free[j % 2], 1)
            for i in range(PT):
                j = T_HEAD + 3 + i
                w = SEQ - i * P
                ve_.wait_ge(t_done, tt + (j + 1))
                d = pb[:, PB_AT[i]:PB_AT[i] + w]
                v.tensor_tensor(d, narrow(j)[:, 0:w], d, ALU.mult).then_inc(t_free[j % 2], 1)
            for i in range(NT):
                j, r = T_HEAD + 7 + i, ROWS[i]
                ve_.wait_ge(t_done, tt + (j + 1))
                d = narrow(j)[0:r, DH:DH + 1]
                step(v.scalar_tensor_tensor(den[0:r, 0, i:i + 1], d, -1.0, ch[0:r, 5 + i:6 + i], ALU.mult, ALU.max))
                step(v.tensor_tensor(den[0:r, 0, i:i + 1], d, den[0:r, 0, i:i + 1], ALU.max))
                step(v.reciprocal(den[0:r, 1, i:i + 1], den[0:r, 0, i:i + 1]))
                v.tensor_scalar(hh[0:r, i, :], narrow(j)[0:r, 0:DH], den[0:r, 1, i:i + 1], None, ALU.mult
                                ).then_inc(t_free[j % 2], 1)
                t_evacuated(ve_, j, 6 * h)
                step(v.bn_stats(hst[0:r, i, :], hh[0:r, i, :]))
            h_evac(ve_, 1, 9 * h)
            v.tensor_copy(ncols[:, 0:8].rearrange("p (c h) -> p c h", c=2)[:, :, bass.ds(h, 1)],
                          cp[:, :, DH:DH + 1]).then_inc(cp_ok, 1)
            for i in range(NT):
                r = ROWS[i]
                last = v.bn_aggr(hmv[0:r, i, :], hst[0:r, i, :])
            step(last)
            v.tensor_scalar(hve[:], hmv[:, :, 1:2].rearrange("p i o -> p (i o)"), EPS, None, ALU.add
                            ).then_inc(var_ok, 1)
            def states(jobs):
                for j in jobs:
                    b, c = (j - 2) // 2, (j - 2) % 2
                    ve_.wait_ge(h_done, th + (j + 1))
                    v.scalar_tensor_tensor(cb[:, b, c, :], cb[:, b, c, :], ch[:, 17 + b:18 + b], third(j)[:, 0:VW],
                                           ALU.mult, ALU.add).then_inc(h_free[j % 2], 1)
            states(range(2, 6))
            ve_.wait_ge(rstd_ok, h + 1)
            for i in range(NT):
                r = ROWS[i]
                last = v.tensor_scalar(hh[0:r, i, :], hh[0:r, i, :], hmv[0:r, i, 0:1], hrs[0:r, i:i + 1],
                                       ALU.subtract, ALU.mult)
            last.then_inc(hn_ok, 1)
            states(range(6, H_PER_HEAD))
            h_evac(ve_, H_PER_HEAD - 1, 9 * h)
            v.tensor_copy(ncols[:, 8:72].rearrange("p (c b h) -> p b c h", c=2, b=DB)[:, :, :, bass.ds(h, 1)],
                          cb[:, :, :, DH:DH + 1]).then_inc(c_upd, 1)
            st.end(H)

        def gated_heads(first, j0):
            for q in range(4):
                ct, j = first + q, j0 + q
                z_evacuated(ve_, j)
                s = sg[ct % 2]
                v.tensor_tensor(s[:], s[:], ht[:, ct, :], ALU.mult).then_inc(hg_ok, 1)
                if q % 2:
                    dense_split_lo(ve_, (C_O, C_O2)[first // 4] + q // 2 + 3)
                ve_.wait_ge(gh_ok, ct + 1)
                v.tensor_tensor(gl[:, ct, :], s[:], gh[:, ct, :].bitcast(F32), ALU.subtract).then_inc(gl_ok, 1)

        gated_heads(0, J_O)
        ve_.wait_ge(c_out, 32 * H)
        ve_.wait_ge(cp_out, 16 * H)
        v.memset(ext[:, :, 0:BUF], 0.0)
        ve_.wait_ge(t_done, T_POOL + 1)
        hist = narrow(T_POOL)[:, 0:NG * DB * BUF].rearrange("p (g b t) -> p g b t", g=NG, b=DB)
        seqs = lambda t, g: t[:, g, BUF + SEQ:EXT].rearrange("p (b t) -> p b t", b=DB)
        for g in range(NG):
            last = v.tensor_copy(seqs(ext, g)[:, :, 0:BUF], hist[:, g])
        last.then_inc(t_free[T_POOL % 2], 1)
        dense_split_lo(ve_, C_U + 3)
        t_evacuated(ve_, T_POOL)
        z_evacuated(ve_, J_U + 2)
        z_evacuated(ve_, J_U + 3)
        v.tensor_copy(po[:, :, 0:BUF], ext[:, :, SEQ:SEQ + BUF])
        for g in range(NG):
            last = v.tensor_copy(po[:, g, BUF:].rearrange("p (b t) -> p b t", b=DB), seqs(ext, g)[:, :, DT:DT + BUF])
        last.then_inc(po_ok, 1)
        step(v.tensor_tensor(sa[:, :, 1:EXT], ext[:, :, 1:EXT], ext[:, :, 0:EXT - 1], ALU.add))
        step(v.tensor_tensor(sbb[:, 1:4, 3:EXT], sa[:, 1:4, 3:EXT], sa[:, 1:4, 1:EXT - 2], ALU.add))
        dense_split_lo(ve_, C_U + 4)
        step(v.tensor_tensor(sa[:, 2:4, 7:EXT], sbb[:, 2:4, 7:EXT], sbb[:, 2:4, 3:EXT - 4], ALU.add))
        step(v.tensor_tensor(sbb[:, 3, 15:EXT], sa[:, 3, 15:EXT], sa[:, 3, 7:EXT - 8], ALU.add))
        first16 = const("first16").rearrange("p (g t) -> p g t", g=NG)
        for g in range(NG):
            s, w = (sa, sbb, sa, sbb)[g], 2.0 ** -(g + 1)
            v.scalar_tensor_tensor(pt[:, g, 16:SEQ], s[:, g, BUF + 16:BUF + SEQ], w, ext[:, g, BUF + 16:BUF + SEQ],
                                   ALU.mult, ALU.subtract)
            v.scalar_tensor_tensor(pt[:, g, SEQ:N].rearrange("p (b t) -> p b t", b=DB), seqs(s, g)[:, :, BUF:], w,
                                   seqs(ext, g)[:, :, BUF:], ALU.mult, ALU.subtract)
            step(v.tensor_tensor(pt[:, g, 0:16], s[:, g, BUF:BUF + 16], first16[:, g], ALU.mult))
            v.tensor_tensor(pt[:, g, 0:16], pt[:, g, 0:16], ext[:, g, BUF:BUF + 16], ALU.subtract
                            ).then_inc(pt_ok, 1)
        ve_.wait_ge(t_done, T_PREV + 1)
        v.tensor_copy(pool_p[:], narrow(T_PREV)[0:BUF, :]).then_inc(t_free[T_PREV % 2], 1)
        ve_.wait_ge(t_done, T_POUT + 1)
        v.tensor_copy(pool_s[:], narrow(T_POUT)[0:DB * BUF, :]).then_inc(t_free[T_POUT % 2], 1)
        ve_.wait_ge(t_done, T_NOUT + 1)
        v.tensor_copy(nrows[:], narrow(T_NOUT)[0:72, 0:P]).then_inc(t_free[T_NOUT % 2], 1)
        gated_heads(4, J_O2)
        for g in range(NG):
            j = J_WP + g
            ve_.wait_ge(pbh_ok, g + 1)
            two = lambda t: t[:, g, :].rearrange("p (a n) -> p a n", a=2)
            v.scalar_tensor_tensor(two(pbl), halves(j), pscale[:, g:g + 1], two(pbh).bitcast(F32), ALU.mult,
                                   ALU.subtract).then_inc(z_free[j % 2], 1)
        dense_split_lo(ve_, C_PB + 3)
        dense_split_lo(ve_, C_PB + 4)
        ve_.wait_ge(z_done, J_MIX)
        v.memset(mxh[:, KT * N:].bitcast(F32), 0.0)
        v.memset(mxl[:, KT * N:].bitcast(F32), 0.0)
        with ve_.Fori(0, 4) as t:
            tz = PER_MIX * t
            for q in range(2):
                dense_split_lo(ve_, C_MIX + 3 + q, t)
            for c in range(2):
                j = J_MIX + 4 + c
                s = sg[c]
                ve_.wait_ge(z_done, tz + (j + 1))
                z_evacuated(ve_, J_MIX + c, 3 * t)
                s2 = s[:].rearrange("p (a n) -> p a n", a=2)
                v.tensor_tensor(s2, halves(j), s2, ALU.mult).then_inc(z_free[j % 2], 1)
                z_evacuated(ve_, j, 3 * t)
                ve_.wait_ge(mt2_ok, 2 * t + (c + 1))
                v.tensor_tensor(s[:], s[:], sg[2 + c][:], ALU.add).then_inc(mix_ok, 1)
            for c in range(2):
                ve_.wait_ge(mxh_ok, 2 * t + (c + 1))
                at = bass.ds((2 * t + c) * N, N)
                v.tensor_tensor(mxl[:, at], sg[c][:], mxh[:, at].bitcast(F32), ALU.subtract).then_inc(mxl_ok, 1)
            dense_split_lo(ve_, C_MIX + 5, t)

        def moe_split_lo(n, hi_count):
            ve_.wait_ge(w_hi, hi_count)
            slot = (C_MOE + n) % SPLIT_SLOTS
            v.tensor_tensor(split_lo[:, slot, :], raw2[:, n % MOE_SLOTS, :], split_hi[:, slot, :].bitcast(F32),
                            ALU.subtract).then_inc(w_lo, 1)

        ve_.wait_ge(x1in, 16 * NT)
        for q in range(4):
            at = slice(256 * q, 256 * q + 256)
            j = J_WO + 2 * q
            ve_.wait_ge(z_done, j + 1)
            v.scalar_tensor_tensor(x1[:, 0:PT, at], x1[:, 0:PT, at], ALPHA,
                                   wide(j).rearrange("p b (q n) -> p (b q) n", q=2), ALU.mult, ALU.add
                                   ).then_inc(z_free[j % 2], 1)
            ve_.wait_ge(z_done, j + 2)
            v.scalar_tensor_tensor(x1[0:NS, PT, at], x1[0:NS, PT, at], ALPHA, wide(j + 1)[0:NS, 0, 0:256], ALU.mult,
                                   ALU.add).then_inc(z_free[(j + 1) % 2], 1)
            if q == 0:
                dense_split_lo(ve_, C_WO + 3)
            elif q < 3:
                moe_split_lo(q - 1, C_MOE + q)
        z_evacuated(ve_, J_WO + 6)
        z_evacuated(ve_, J_WO + 7)

        def row_stats(i, var_sem):
            r = ROWS[i]
            for q in range(2):
                last = v.bn_stats(lst[0:r, i, q, :], x1[0:r, i, 512 * q:512 * q + 512])
            step(last)
            step(v.bn_aggr(hmv[0:r, i, :], lst[0:r, i].rearrange("p q s -> p (q s)")))
            v.tensor_scalar(hve[0:r, i:i + 1], hmv[0:r, i, 1:2], EPS, None, ALU.add).then_inc(var_sem, 1)

        def row_shift(i, rstd_sem, out_sem):
            r = ROWS[i]
            ve_.wait_ge(rstd_sem, i + 1)
            v.scalar_tensor_tensor(hnm[0:r, i:i + 1], hmv[0:r, i, 0:1], -1.0, hrs[0:r, i:i + 1], ALU.mult, ALU.mult
                                   ).then_inc(out_sem, 1)

        def row_bias(i, in_sem, out_sem):
            r = ROWS[i]
            ve_.wait_ge(in_sem, i + 1)
            v.tensor_tensor(x1[0:r, i, :], x1[0:r, i, :], lnb[0:r, :], ALU.add).then_inc(out_sem, 1)

        ve_.wait_ge(ln_in, 32)
        for i in range(NT + 2):
            if i < NT:
                row_stats(i, lv_ok)
            if 1 <= i <= NT:
                row_shift(i - 1, lr_ok, lc_ok)
            if i >= 2:
                row_bias(i - 2, lg_ok, x1_ok)
        moe_split_lo(2, C_MOE + 3)

        v.memset(lg[:], 0.0)
        v.tensor_copy(tok_bf[:], const("tokid"))
        step(v.memset(zero16[:], 0.0))
        ve_.wait_ge(t_done, T_LOGIT + 1)
        logits = narrow(T_LOGIT)[:, 0:NT * NE].rearrange("p (i e) -> p i e", i=NT)
        v.tensor_tensor(lg[:, 0:PT, :], logits[:, 0:PT, :], bc(brt[:], 1, [P, PT, NE]), ALU.add)
        v.tensor_tensor(lg[0:NS, PT, :], logits[0:NS, PT, :], brt[0:NS, :], ALU.add).then_inc(t_free[T_LOGIT % 2], 1)
        t_evacuated(ve_, T_LOGIT)
        mx = rsm[:, 0, 0:NT]
        step(v.tensor_reduce(mx, lg[:], AX.X, ALU.max))
        v.tensor_tensor(lg[:], lg[:], bc(mx, 2, [P, NT, NE]), ALU.subtract).then_inc(sh_ok, 1)
        ve_.wait_ge(se_ok, 1)
        step(v.tensor_reduce(rsm[:, 1, 0:NT], pr[:], AX.X, ALU.add))
        step(v.reciprocal(rsm[:, 0, 0:NT], rsm[:, 1, 0:NT]))
        step(v.tensor_tensor(pr[:], pr[:], bc(rsm[:, 0, 0:NT], 2, [P, NT, NE]), ALU.mult))

        def rank(out, tmp, val, groups):
            step(v.tensor_tensor(out[:, :, 1:4], val[:, :, 0:1].to_broadcast([P, groups, 3]), val[:, :, 1:4],
                                 ALU.is_ge))
            step(v.memset(out[:, :, 0:1], 0.0))
            for k in range(1, 4):
                v.tensor_tensor(tmp[:, :, 0:k + 1], val[:, :, k:k + 1].to_broadcast([P, groups, k + 1]),
                                val[:, :, 0:k + 1], ALU.is_gt)
                if k < 3:
                    v.tensor_tensor(tmp[:, :, k + 1:4], val[:, :, k:k + 1].to_broadcast([P, groups, 3 - k]),
                                    val[:, :, k + 1:4], ALU.is_ge)
                step(v.tensor_copy(rsm[:, 5, 0:1], rsm[:, 0, 0:1]))
                step(v.tensor_tensor(out, out, tmp, ALU.add))

        by4 = lambda t: t[:].rearrange("p i (g e) -> p (i g) e", e=4)
        rank(by4(rk), by4(tmp_r), by4(pr), NT * EG)
        step(v.tensor_scalar(sel[:], rk[:], 1.5, None, ALU.is_lt))
        step(v.tensor_tensor(tmp_r[:], pr[:], sel[:], ALU.mult))
        gsc, grk, gtm = (rsm[:, q, :] for q in (1, 2, 3))
        step(v.tensor_reduce(gsc, by4(tmp_r), AX.X, ALU.add))
        g4 = lambda t: t.rearrange("p (i g) -> p i g", g=EG)
        rank(g4(grk), g4(gtm), g4(gsc), NT)
        step(v.tensor_scalar(gtm, grk, 0.5, None, ALU.is_lt))
        step(v.tensor_tensor(by4(sel), by4(sel), bc(gtm, 2, [P, NT * EG, 4]), ALU.mult))
        v.tensor_tensor(sel[:], sel[:], bc(const("valid"), 2, [P, NT, NE]), ALU.mult).then_inc(sel_ok, 1)
        ve_.wait_ge(sel_ok, 1)
        ve_.wait_ge(t_done, T_POS + 1)
        step(v.tensor_copy(pos[:], narrow(T_POS)[:, 0:NT * NE].rearrange("p (i e) -> p i e", i=NT)))
        step(v.scalar_tensor_tensor(tmp_r[:], pos[:], 1.0, sel[:], ALU.add, ALU.mult))
        step(v.tensor_scalar(tmp_r[:], tmp_r[:], -1.0, None, ALU.add))
        for i in range(NT):
            v.tensor_tensor(onehot[:, i], bc(const("slot"), 1, [P, NE, P]), bc(tmp_r[:, i, :], 2, [P, NE, P]),
                            ALU.is_equal).then_inc(oh_ok, 1)
        step(v.tensor_tensor(gate[:], pr[:], sel[:], ALU.mult))
        step(v.tensor_reduce(rsm[:, 0, 0:NT], gate[:], AX.X, ALU.add))
        step(v.tensor_scalar(rsm[:, 0, 0:NT], rsm[:, 0, 0:NT], 1e-37, None, ALU.max))
        step(v.reciprocal(rsm[:, 4, 0:NT], rsm[:, 0, 0:NT]))
        step(v.tensor_tensor(gate[:], gate[:], bc(rsm[:, 4, 0:NT], 2, [P, NT, NE]), ALU.mult))
        step(v.tensor_scalar(s1[:], rk[:], 0.5, None, ALU.is_lt))
        step(v.tensor_tensor(s1[:], s1[:], sel[:], ALU.mult))
        step(v.tensor_tensor(tmp_r[:], gate[:], s1[:], ALU.mult))
        step(v.tensor_reduce(gates_ab[:, 0, :], tmp_r[:], AX.X, ALU.add))
        step(v.tensor_tensor(rk[:], sel[:], s1[:], ALU.subtract))
        step(v.tensor_tensor(tmp_r[:], gate[:], rk[:], ALU.mult))
        step(v.tensor_reduce(gates_ab[:, 1, :], tmp_r[:], AX.X, ALU.add))
        ve_.wait_ge(t_done, T_IDX + 1)
        step(v.tensor_copy(idx_f[:], narrow(T_IDX)[:, 0:2 * NE]))
        pair = idx_f[:].rearrange("p (e q) -> p e q", q=2)
        v.scalar_tensor_tensor(idx_i[:].unsqueeze(2), pair[:, :, 1:2], float(P), pair[:, :, 0:1], ALU.mult, ALU.add
                               ).then_inc(idx_ok, 1)
        ve_.wait_ge(t_done, T_CNT + 1)
        step(v.tensor_copy(cnt_v[:], narrow(T_CNT)[:, 0:NE]))
        step(v.tensor_scalar(ovf[:], cnt_v[:], float(P), None, ALU.is_gt))
        for k in range(2, 5):
            step(v.scalar_tensor_tensor(ovf[:], cnt_v[:], float(P * k), ovf[:], ALU.is_gt, ALU.add))
        step(v.tensor_tensor_scan(incl[:], ovf[:], zero16[:], 0.0, ALU.add, ALU.add))
        step(v.tensor_tensor(obase[:], incl[:], ovf[:], ALU.subtract))
        step(v.tensor_tensor(obase[:], obase[:], const("expert"), ALU.subtract))
        step(v.tensor_scalar(obase[:], obase[:], 15.0, None, ALU.add))
        step(v.tensor_scalar(dest[:], pos[:], float(P), None, ALU.is_ge))
        step(v.tensor_tensor(dest[:], dest[:], bc(obase[:], 1, [P, NT, NE]), ALU.mult))
        step(v.tensor_tensor(dest[:], dest[:], bc(const("expert"), 1, [P, NT, NE]), ALU.add))
        step(v.scalar_tensor_tensor(dest[:], dest[:], float(P), pos[:], ALU.mult, ALU.add))
        for a, s_ in enumerate((s1, rk)):
            step(v.tensor_tensor(tmp_r[:], dest[:], s_[:], ALU.mult))
            step(v.tensor_reduce(dest_f[:, a, :], tmp_r[:], AX.X, ALU.add))
        v.tensor_copy(dest_i[:], dest_f[:])
        step(v.tensor_tensor(ovx[:], bc(incl[:], 1, [P, XTRA, NE]), bc(const("block"), 2, [P, XTRA, NE]), ALU.is_le))
        step(v.tensor_reduce(cnt_v[:, 0:XTRA], ovx[:], AX.X, ALU.add))
        step(v.tensor_scalar(cnt_v[:, 0:XTRA], cnt_v[:, 0:XTRA], float(NE - 1), None, ALU.min))
        step(v.tensor_copy(cnt_v[:, XTRA:XTRA + 1], incl[:, NE - 1:NE]))
        v.tensor_copy(ctl[:], cnt_v[:, 0:XTRA + 1]).then_inc(xa_ok, 1)

        def x_low():
            v.tensor_tensor(xgl[:], wide(0).rearrange("p b (q t) -> p (b q) t", q=4), xgh[:].bitcast(F32),
                            ALU.subtract).then_inc(xgl_ok, 1)

        def silu(done):
            ve_.wait_ge(sig_ok, done + 1)
            ve_.wait_ge(dve, st.mark(v.tensor_tensor(gs[:], psum[:, 2, :], gs[:], ALU.mult)))

        def times_up():
            v.tensor_tensor(hs[:], psum[:, 3, :], gs[:], ALU.mult).then_inc(hs_ok, 1)

        def h_low():
            v.tensor_tensor(htl[:], psum[:, 6, :].rearrange("p (q t) -> p q t", q=4), hth[:].bitcast(F32),
                            ALU.subtract).then_inc(htl_ok, 1)

        def store_half():
            v.tensor_copy(ys[:, 512:DM], psum[:, 5, :]).then_inc(yd_ok, 1)

        ve_.wait_ge(xgh_ok, 1)
        x_low()
        for n in range(4):
            moe_split_lo(n + 3, C_MOE + n + 4)
            if n == 1:
                silu(0)
        ve_.wait_ge(w_used, 4)
        times_up()
        ve_.wait_ge(xgh_ok, 2)
        x_low()
        ve_.wait_ge(hth_ok, 1)
        h_low()

        def turn(e, last=False):
            for j in range(6):
                if j == 4:
                    ve_.wait_ge(w_used, 6 * e + 2)
                    times_up()
                    if not last:
                        ve_.wait_ge(xgh_ok, e + 2)
                        x_low()
                if j < 5 or not last:
                    moe_split_lo(7 + j, 6 * e + (C_MOE + 7 + j + 1 - 6))
                if j == 2:
                    silu(e)
            ve_.wait_ge(w_used, 6 * e + 4)
            ve_.wait_ge(y_out, 16 * e + 16)
            store_half()
            ve_.wait_ge(hth_ok, e + 1)
            h_low()

        with ve_.Fori(1, NE - 1) as e:
            st.loop(e - 1, 1)
            turn(e)
            st.end(NE - 2)
        turn(NE - 1, last=True)
        ve_.wait_ge(w_used, 6 * NE)
        ve_.wait_ge(y_out, 16 * (NE + 1))
        store_half()
        extra = ve_.value_load(ctl[0:1, XTRA:XTRA + 1], min_val=0, max_val=XTRA)
        with ve_.Fori(0, XTRA) as j:
            st.loop(j, 5)
            with ve_.If(extra > j):
                bx = rsx[:, 0:1]
                step(v.tensor_copy(bx, const("block")[:, bass.ds(j, 1)]))
                step(v.tensor_scalar(bx, bx, float(P), float(NE * P), ALU.mult, ALU.add))
                step(v.tensor_scalar(dx[:], dest_f[:], bx, None, ALU.subtract))
                for a in range(2):
                    last = v.tensor_tensor(oh2[:, a], bc(const("slot"), 1, [P, NT, P]), bc(dx[:, a, :], 2, [P, NT, P]),
                                           ALU.is_equal)
                last.then_inc(oh2_ok, 1)
                ve_.wait_ge(ix2_done, j + 1)
                step(v.tensor_copy(idx_f[:, 0:2], narrow(1)[:, 0:2]))
                v.scalar_tensor_tensor(idx_c[:], idx_f[:, 1:2], float(P), idx_f[:, 0:1], ALU.mult, ALU.add
                                       ).then_inc(ix2_ok, 1)
                ve_.wait_ge(xgh_ok, j + (NE + 1))
                x_low()
                for m in range(6):
                    moe_split_lo(m, 6 * j + (C_MOE + 97 + m))
                    if m == 3:
                        silu(j + NE)
                        ve_.wait_ge(w_used, 6 * j + 100)
                        times_up()
                        ve_.wait_ge(hth_ok, j + (NE + 1))
                        h_low()
                ve_.wait_ge(w_used, 6 * j + 102)
                store_half()
            ve_.nop()
            st.end(XTRA)

        def combine(i):
            r = ROWS[i]
            ve_.wait_ge(yg_in[i], 32)
            ve_.wait_ge(xal_ok, i + 1)
            step2(v.scalar_tensor_tensor(x1[0:r, i, :], ya[0:r, i, :], gates_ab[0:r, 0, i:i + 1], x1[0:r, i, :],
                                         ALU.mult, ALU.add))
            step2(v.scalar_tensor_tensor(x1[0:r, i, :], ybk[0:r, i, :], gates_ab[0:r, 1, i:i + 1], x1[0:r, i, :],
                                         ALU.mult, ALU.add))

        tail = Steps(dve_tail)

        def step2(ins):
            ve_.wait_ge(dve_tail, tail.mark(ins))

        st = tail
        step = step2
        for i in range(NT + 2):
            if i < NT:
                combine(i)
                r = ROWS[i]
                for q in range(2):
                    last = v.bn_stats(lst[0:r, i, q, :], x1[0:r, i, 512 * q:512 * q + 512])
                step2(last)
                step2(v.bn_aggr(hmv[0:r, i, :], lst[0:r, i].rearrange("p q s -> p (q s)")))
                v.tensor_scalar(hve[0:r, i:i + 1], hmv[0:r, i, 1:2], EPS, None, ALU.add).then_inc(v2_ok, 1)
            if 1 <= i <= NT:
                row_shift(i - 1, r2_ok, c2_ok)
            if i >= 2:
                row_bias(i - 2, g2_ok, fin_ok)

    @block.tensor
    def _(pe):
        mm = nc.tensor.matmul
        ident = const("ident")

        def chunk(c, k, a, n, kk=KT):
            slot, w = c % SPLIT_SLOTS, CHUNK // kk
            at = slice(k * w + a, k * w + a + n)
            return split_hi[:, slot, at], split_lo[:, slot, at]

        pe.wait_ge(cst_in, 16)
        for i in range(NT):
            r, j = ROWS[i], J_X + i
            pe.wait_ge(x_in[i], 16)
            if j >= 2:
                z_room(pe, j)
            out = wide(j).rearrange("p b (q t) -> p (b q) t", q=4)
            for k in range(KT):
                last = nc.tensor.transpose(out[:, k, 0:r], xn[0:r, i, whole(k)], ident[0:r, 0:r])
            last.then_inc(z_done, 1)
        z_evacuated(pe, J_X + 3)
        z_evacuated(pe, J_X + 4)
        pe.wait_ge(wgl_ok, 1)
        for q, j in enumerate((J_LI, J_LF)):
            z_room(pe, j)
            for a in range(2):
                for k in range(KT):
                    last = product3(halves(j)[:, a, :], wg_hi[:, q, k, :], wg_lo[:, q, k, :],
                                    xcols(x_hi, k, a * HALF, HALF), xcols(x_lo, k, a * HALF, HALF), k == 0,
                                    k == KT - 1)
            last.then_inc(z_done, 1)
        pe.wait_ge(em_ok, 3)
        for q, row in enumerate((g_r, em, w_r)):
            for i in range(NT):
                r = ROWS[i]
                at = (q * NT + i) * H
                last = nc.tensor.transpose(narrow(T_COL)[0:r, at:at + H], row[:, i * P:i * P + r], ident[0:H, 0:H])
        last.then_inc(t_done, 1)
        head_sel = const("head_sel", H)
        for h in range(H):
            at = h * (NS + DB)
            last = mm(narrow(T_SIL)[:, at:at + NS + DB], head_sel[:, whole(h)], sil[:], start=True, stop=True)
        last.then_inc(t_done, 1)
        pe.wait_ge(nn_in, 16)
        t_room(pe, T_N)
        for c in range(2):
            last = nc.tensor.transpose(narrow(T_N)[:, c * NS:c * NS + NS], nn[:, whole(c)], ident[0:NS, 0:NS])
        last.then_inc(t_done, 1)
        for h in range(H):
            j = J_BM + h
            z_room(pe, j)
            for a in range(2):
                last = mm(halves(j)[:, a, :], head_sel[:, whole(h)], nm[:, a * HALF:(a + 1) * HALF], start=True,
                          stop=True)
            last.then_inc(z_done, 1)
        pe.wait_ge(ready, H)

        def project(j, c, col_, rhs_hi, rhs_lo, kk=KT, more=0):
            z_room(pe, j, more)
            for a in range(2):
                for k in range(kk):
                    w_h, w_l = chunk(c, k, col_, P, kk)
                    last = product3(halves(j)[:, a, :], w_h, w_l, xcols(rhs_hi, k, a * HALF, HALF),
                                    xcols(rhs_lo, k, a * HALF, HALF), k == 0, k == kk - 1)
            last.then_inc(z_done, 1)

        with pe.Fori(0, H) as h:
            z0, mz, mt_, mh = J_HEAD, 4 * h, 6 * h, 9 * h
            for q in range(2):
                pe.wait_ge(w_lo, 3 * h + (q + 1))
                for c in range(2):
                    project(z0 + 2 * q + c, q, c * P, x_hi, x_lo, KT, mz)
            pe.wait_ge(w_lo, 3 * h + 3)
            for i in range(NT):
                j = z0 + 4 + i // PT
                if i % PT == 0:
                    z_room(pe, j, mz)
                out = wide(j).rearrange("p b (q n) -> p (b q) n", q=2)[:, i % PT, :]
                for k in range(KT):
                    w_h, w_l = chunk(2, k, 0, DH)
                    last = product3(out, xcols(x_hi, k, i * P, P), xcols(x_lo, k, i * P, P), w_h, w_l, k == 0,
                                    k == KT - 1)
                if i >= PT - 1:
                    last.then_inc(z_done, 1)
            z_evacuated(pe, z0 + 2, mz)
            z_evacuated(pe, z0 + 3, mz)
            for q in range(3):
                j = T_HEAD + q
                t_room(pe, j, mt_)
                for i in range(2 * q, min(2 * q + 2, NT)):
                    r = ROWS[i]
                    for c in range(2):
                        at = (i % 2) * DH + c * P
                        last = nc.tensor.transpose(narrow(j)[0:r, at:at + P], kt[:, c, i * P:i * P + r], ident)
                if q == 2:
                    z_evacuated(pe, z0, mz)
                    z_evacuated(pe, z0 + 1, mz)
                    for c in range(2):
                        last = mm(narrow(j)[0:NS, DH:DH + NS], kt[:, c, SEQ:N], qt[:, c, SEQ:N], start=c == 0,
                                  stop=c == 1)
                last.then_inc(t_done, 1)
            for i in range(PT):
                j = T_HEAD + 3 + i
                t_room(pe, j, mt_)
                for c in range(2):
                    last = mm(narrow(j)[:, 0:SEQ - i * P], kt[:, c, i * P:i * P + P], qt[:, c, i * P:SEQ],
                              start=c == 0, stop=c == 1)
                last.then_inc(t_done, 1)
            z_evacuated(pe, z0 + 4, mz)
            t_evacuated(pe, T_HEAD + 1, mt_)
            for c in range(2):
                h_room(pe, c, mh)
                for i in range(PT):
                    last = mm(third(c)[:, 0:VW], kw[:, i, whole(c)], ve[:, i, :], start=i == 0, stop=i == PT - 1)
                last.then_inc(h_done, 1)
            for t in range(PT):
                j = T_HEAD + 7 + t
                t_room(pe, j, mt_)
                t_evacuated(pe, T_HEAD + 3 + t, mt_)
                for i in range(t + 1):
                    at = PB_AT[i] + (t - i) * P
                    last = mm(narrow(j)[:, 0:VW], pb[:, at:at + P], ve[:, i, :], start=i == 0, stop=i == t)
                last.then_inc(t_done, 1)
            j = T_HEAD + 11
            t_room(pe, j, mt_)
            pe.wait_ge(n_ok, h + 1)
            pe.wait_ge(qm_ok, h + 1)
            z_evacuated(pe, z0 + 5, mz)
            for b in range(DB):
                for c in range(2):
                    mm(narrow(j)[0:NS, 0:VW], qm[:, c, b, :], cb[:, b, c, :], start=b + c == 0, stop=False)
            mm(narrow(j)[0:NS, 0:VW], ps_[:], ve[0:NS, PT, :], start=False, stop=True).then_inc(t_done, 1)
            for b in range(DB):
                for c in range(2):
                    jh = 2 + 2 * b + c
                    h_room(pe, jh, mh)
                    mm(third(jh)[:, 0:VW], kwm[:, b, whole(c)], ve[0:NS, PT, :], start=True, stop=True
                       ).then_inc(h_done, 1)
            pe.wait_ge(hn_ok, h + 1)
            for c in range(2):
                j = z0 + 6 + c
                z_room(pe, j, mz)
                for i in range(NT):
                    r = ROWS[i]
                    out = wide(j)[:, 0, i * P:i * P + P] if i < PT else wide(j)[:, 1, 0:NS]
                    last = nc.tensor.transpose(out, hh[0:r, i, whole(c)], ident[0:r, 0:r])
                last.then_inc(z_done, 1)

        def projections(j0, c0, chunks, hi, lo):
            for q in range(chunks):
                pe.wait_ge(w_lo, c0 + q + 1)
                for c in range(2):
                    project(j0 + 2 * q + c, c0 + q, c * P, hi, lo)

        projections(J_O, C_O, 2, x_hi, x_lo)
        projections(J_U, C_U, 2, x_hi, x_lo)
        pe.wait_ge(spn_in, 16)
        t_room(pe, T_POOL)
        rows = DB * BUF
        for g in range(NG):
            last = nc.tensor.transpose(narrow(T_POOL)[:, g * rows:(g + 1) * rows], spn[:, whole(g)],
                                       ident[0:rows, 0:rows])
        last.then_inc(t_done, 1)
        projections(J_O2, C_O2, 1, x_hi, x_lo)
        pe.wait_ge(po_ok, 1)
        for j, a, n in ((T_PREV, 0, BUF), (T_POUT, BUF, rows)):
            t_room(pe, j)
            for g in range(NG):
                last = nc.tensor.transpose(narrow(j)[0:n, whole(g)], po[:, g, a:a + n], ident)
            last.then_inc(t_done, 1)
        t_room(pe, T_NOUT)
        pe.wait_ge(c_upd, H)
        nc.tensor.transpose(narrow(T_NOUT)[0:72, 0:P], ncols[:], ident).then_inc(t_done, 1)
        projections(J_O2 + 2, C_O2 + 1, 1, x_hi, x_lo)
        pe.wait_ge(wp_in, 16)
        for g in range(NG):
            j = J_WP + g
            z_room(pe, j)
            pe.wait_ge(pt_ok, g + 1)
            for a in range(2):
                last = mm(halves(j)[:, a, :], wp[:, g, :], pt[:, g, a * HALF:(a + 1) * HALF], start=True, stop=True)
            last.then_inc(z_done, 1)
        z_evacuated(pe, J_WP + 2)
        z_evacuated(pe, J_WP + 3)
        pb_hi, pb_lo = (t[:].rearrange("p g n -> p (g n)") for t in (pbh, pbl))
        for ct in range(KT):
            c = C_PB + ct // 4
            pe.wait_ge(w_lo, c + 1)
            project(J_PB + ct, c, (ct % 4) * P, pb_hi, pb_lo, 4)
        g_hi, g_lo = (t[:].rearrange("p g n -> p (g n)") for t in (gh, gl))
        pe.wait_ge(gl_ok, KT)
        with pe.Fori(0, 4) as t:
            for q in range(3):
                pe.wait_ge(w_lo, 3 * t + (C_MIX + q + 1))
                for c in range(2):
                    hi, lo = (g_hi, g_lo) if q == 2 else (x_hi, x_lo)
                    project(J_MIX + 2 * q + c, C_MIX + q, c * P, hi, lo, KT, 3 * t)
        pe.wait_ge(mxl_ok, KT)
        for q in range(4):
            pe.wait_ge(w_lo, C_WO + q + 1)
            for i in range(NT):
                j = J_WO + 2 * q + i // PT
                if i % PT == 0:
                    z_room(pe, j)
                out = wide(j).rearrange("p b (q n) -> p (b q) n", q=2)[:, i % PT, :]
                for k in range(KT):
                    w_h, w_l = chunk(C_WO + q, k, 0, 256)
                    last = product3(out, xcols(mxh, k, i * P, P), xcols(mxl, k, i * P, P), w_h, w_l, k == 0,
                                    k == KT - 1)
                if i >= PT - 1:
                    last.then_inc(z_done, 1)
        for i in range(NT):
            r, j = ROWS[i], J_XT + i
            pe.wait_ge(x1_ok, i + 1)
            z_room(pe, j)
            out = wide(j).rearrange("p b (q t) -> p (b q) t", q=4)
            for k in range(KT):
                last = nc.tensor.transpose(out[:, k, 0:r], x1[0:r, i, whole(k)], ident[0:r, 0:r])
            last.then_inc(z_done, 1)
        pe.wait_ge(wr_in, 16)
        t_room(pe, T_LOGIT)
        for i in range(NT):
            r = ROWS[i]
            z_evacuated(pe, J_XT + i)
            for k in range(KT):
                last = mm(narrow(T_LOGIT)[0:r, i * NE:(i + 1) * NE], x1t[:, k, i * P:i * P + r], wr[:, k, :],
                          start=k == 0, stop=k == KT - 1)
        last.then_inc(t_done, 1)
        pe.wait_ge(sel_ok, 1)
        for i in range(NT):
            out = narrow(T_POS)[:, i * NE:(i + 1) * NE]
            for k in range(i):
                mm(out, const("ones"), sel[:, k, :], start=k == 0, stop=False)
            last = mm(out, const("before"), sel[:, i, :], start=i == 0, stop=True)
        last.then_inc(t_done, 1)
        t_evacuated(pe, T_LOGIT)
        for i in range(NT):
            last = mm(narrow(T_CNT)[:, 0:NE], const("ones"), sel[:, i, :], start=i == 0, stop=i == NT - 1)
        last.then_inc(t_done, 1)
        pe.wait_ge(oh_ok, NT)
        for e in range(NE):
            for i in range(NT):
                last = mm(narrow(T_IDX)[:, 2 * e:2 * e + 2], onehot[:, i, e, :], tok_bf[:, 2 * i:2 * i + 2],
                          start=i == 0, stop=i == NT - 1)
        last.then_inc(t_done, 1)

        def rows_in():
            out = wide(0).rearrange("p b (q t) -> p (b q) t", q=4)
            for k in range(KT):
                last = nc.tensor.transpose(out[:, k, :], xg[:, whole(k)], ident)
            last.then_inc(xt_done, 1)

        def up(n, bank, half):
            for k in range(4):
                w_h, w_l = chunk(C_MOE + n, k, 0, DE, 4)
                kk = 4 * half + k
                last = product3(psum[:, bank, :], xgh[:, kk, :], xgl[:, kk, :], w_h, w_l, kk == 0, kk == KT - 1)
            last.then_inc(w_used, 1)

        def down(n, half):
            for k in range(4):
                w_h, w_l = chunk(C_MOE + n, k, 0, 512, 4)
                last = product3(psum[:, 4 + half, :], hth[:, k, :], htl[:, k, :], w_h, w_l, k == 0, k == 3)
            last.then_inc(w_used, 1)

        def hidden_in():
            for k in range(4):
                last = nc.tensor.transpose(psum[:, 6, k * P:(k + 1) * P], hs[:, whole(k)], ident)
            last.then_inc(hi_done, 1)

        pe.wait_ge(g_in, 16)
        rows_in()
        pe.wait_ge(xgl_ok, 1)
        for n in range(4):
            pe.wait_ge(w_lo, C_MOE + n + 1)
            up(n, 2 + n // 2, n % 2)
        pe.wait_ge(g_in, 32)
        rows_in()
        pe.wait_ge(hs_ok, 1)
        hidden_in()

        def turn(e, last=False):
            pe.wait_ge(xgl_ok, e + 1)
            for j in range(4):
                pe.wait_ge(w_lo, 6 * e + (C_MOE + 4 + j + 1 - 6))
                up(4 + j, 2 + j // 2, j % 2)
            if not last:
                pe.wait_ge(g_in, 16 * e + 32)
                rows_in()
            pe.wait_ge(htl_ok, e)
            if last:
                pe.wait_ge(yd_ok, e - 1)
                pe.wait_ge(ya_ok, e - 1)
            else:
                pe.wait_ge(yd_ok, e - 1)
                pe.wait_ge(ya_ok, e - 1)
            for j in range(4, 6):
                pe.wait_ge(w_lo, 6 * e + (C_MOE + 4 + j + 1 - 6))
                down(4 + j, j - 4)
            pe.wait_ge(hs_ok, e + 1)
            hidden_in()

        with pe.Fori(1, NE - 1) as e:
            turn(e)
        turn(NE - 1, last=True)
        pe.wait_ge(htl_ok, NE)
        pe.wait_ge(yd_ok, NE - 1)
        pe.wait_ge(ya_ok, NE - 1)
        for j in range(2):
            pe.wait_ge(w_lo, C_MOE + 95 + j)
            down(94 + j, j)
        extra = pe.value_load(ctl[0:1, XTRA:XTRA + 1], min_val=0, max_val=XTRA)
        with pe.Fori(0, XTRA) as j:
            with pe.If(extra > j):
                pe.wait_ge(oh2_ok, j + 1)
                for a in range(2):
                    for i in range(NT):
                        last = mm(narrow(1)[:, 0:2], oh2[:, a, i, :], tok_bf[:, 2 * i:2 * i + 2],
                                  start=a == 0 and i == 0, stop=a == 1 and i == NT - 1)
                last.then_inc(ix2_done, 1)
                pe.wait_ge(g_in, 16 * j + 16 * (NE + 1))
                rows_in()
                pe.wait_ge(xgl_ok, j + (NE + 1))
                for m in range(4):
                    pe.wait_ge(w_lo, 6 * j + (C_MOE + 97 + m))
                    up(m, 2 + m // 2, m % 2)
                pe.wait_ge(hs_ok, j + (NE + 1))
                hidden_in()
                pe.wait_ge(htl_ok, j + (NE + 1))
                pe.wait_ge(yd_ok, j + NE)
                pe.wait_ge(ya_ok, j + NE)
                for m in range(4, 6):
                    pe.wait_ge(w_lo, 6 * j + (C_MOE + 97 + m))
                    down(m, m - 4)
            pe.nop()


_INS = ["x_prompt", "x_sample", "state_C", "state_n", "state_m", "state_pool", "w_in", "b_gate", "hn_gain", "w_pool",
        "pool_scale", "w_proj_a", "w_proj_b", "w_out", "ln1_g", "ln1_b", "ln2_g", "ln2_b", "w_router", "b_router",
        "w_e_gate", "w_e_up", "w_e_down"]
_OUTS = [(1, SEQ, DM), (DB, DT, DM), (1, 1, H, DH, DH), (1, 1, H, DH), (1, 1, H), (1, 1, BUF, NG * GD),
         (1, DB, H, DH, DH), (1, DB, H, DH), (1, DB, H), (1, DB, BUF, NG * GD)]


def _constants():
    import numpy as np

    c = np.zeros((P, CW), np.float32)
    p, f = np.arange(P)[:, None], np.arange(P)[None, :]

    def put(name, value):
        a, w = CONST[name]
        c[:, a:a + w] = np.broadcast_to(value, (P, w))

    s = np.arange(NS)[None, :]
    put("ident", p == f)
    put("causal", np.where(p <= f, 0.0, FAR))
    put("causal_s", np.where((p // DT == s // DT) & (p <= s), 0.0, FAR))
    put("seq_of", (np.arange(DB)[:, None] == np.arange(NS)[None, :] // DT).reshape(1, -1))
    put("head_sel", (p == np.arange(H * P)[None, :] // P))
    put("tok_seq", (p // DT == np.arange(DB)[None, :]))
    put("first16", np.concatenate([1.0 / np.minimum(np.arange(16) + 1, 2 << g) for g in range(NG)])[None, :])
    put("before", p < f)
    put("ones", 1.0)
    put("slot", f)
    put("tokid", np.stack([np.broadcast_to(p, (P, NT)), np.broadcast_to(np.arange(NT)[None, :], (P, NT))],
                          2).reshape(P, -1))
    put("expert", np.arange(NE)[None, :])
    put("valid", np.arange(NT)[None, :] * P + p < N)
    put("block", np.arange(XTRA)[None, :])
    put("half", -0.5)
    return c


def kernel(**inputs):
    import numpy as _np
    import concourse.bacc as _bacc
    from concourse import mybir as _mybir
    from concourse.bass_utils import run_bass_kernel_spmd as _run

    nc = _bacc.Bacc("TRN2", target_bir_lowering=False, num_devices=1)
    arrays, args = {}, []
    for name, a in [("consts", _constants())] + [(n, _np.ascontiguousarray(inputs[n])) for n in _INS]:
        arrays[f"in_{name}_dram"] = a
        args.append(nc.dram_tensor(f"in_{name}_dram", a.shape, _mybir.dt.from_np(a.dtype), kind="ExternalInput").ap())
    for i, shape in enumerate(_OUTS):
        args.append(nc.dram_tensor(f"out_{i}_dram", shape, F32, kind="ExternalOutput").ap())
    build(nc, *args)
    r = _run(nc, [arrays], core_ids=[0])
    return tuple(r.results[0][f"out_{i}_dram"] for i in range(len(_OUTS)))
```
